# Optimizing a Trainium2 kernel written in Bass

```python
import math
import jax, jax.numpy as jnp
from jax import lax
import numpy as np

D_MODEL = 1024
BATCH = 1
SEQ = 1024
DEPTH = 1

HEAD_DIM = 64
FOX_HEADS = 8
FOX_WIDTH = FOX_HEADS * HEAD_DIM
MLSTM_HEADS = 8
MLSTM_QK_DIM = 32
MLSTM_V_DIM = 64
MLSTM_QK_WIDTH = MLSTM_HEADS * MLSTM_QK_DIM
MLSTM_V_WIDTH = MLSTM_HEADS * MLSTM_V_DIM
MIX_WIDTH = FOX_WIDTH + MLSTM_V_WIDTH
CONV_WIDTH = 4
FOX_BLOCK = 128
MLSTM_CHUNK = 64
SPLIT_WIDTHS = (FOX_WIDTH, FOX_WIDTH, FOX_WIDTH, FOX_HEADS,
                MLSTM_QK_WIDTH, MLSTM_QK_WIDTH, MLSTM_V_WIDTH,
                MLSTM_HEADS, MLSTM_HEADS, MLSTM_V_WIDTH)
IN_PROJ_WIDTH = sum(SPLIT_WIDTHS)
N_EXPERTS = 32
TOP_K = 4
D_EXPERT = D_MODEL
SWIGLU_ALPHA = 1.702
SWIGLU_LIMIT = 7.0
MOE_BLOCK = 128
NORM_EPS = 1e-5

kernel_name = "hymba_fox_mlstm_moe_layer"

def rms_norm(x, w):
    xf = x.astype(jnp.float32)
    y = xf * lax.rsqrt(jnp.mean(xf * xf, axis=-1, keepdims=True) + NORM_EPS)
    return (y * w.astype(jnp.float32)).astype(x.dtype)

def to_heads(t, n_heads):
    b, s, w = t.shape
    return t.reshape(b, s, n_heads, w // n_heads).transpose(0, 2, 1, 3)

def head_group_norm(t, w):
    b, h, s, d = t.shape
    tf = t.astype(jnp.float32)
    tf = tf * lax.rsqrt(jnp.mean(tf * tf, axis=-1, keepdims=True) + NORM_EPS)
    return tf.transpose(0, 2, 1, 3).reshape(b, s, h * d) * w.astype(jnp.float32)

def causal_depthwise_conv(u, w):
    c = u.shape[-1]
    return lax.conv_general_dilated(
        u, w.astype(u.dtype)[:, None, :], window_strides=(1,),
        padding=[(CONV_WIDTH - 1, 0)], dimension_numbers=('NWC', 'WIO', 'NWC'),
        feature_group_count=c)

def forgetting_attention(q, k, v, log_f):
    seq = q.shape[2]
    cum = jnp.cumsum(log_f, axis=-1)
    scale = 1.0 / math.sqrt(HEAD_DIM)
    outs = []
    for blk in range(seq // FOX_BLOCK):
        start, end = blk * FOX_BLOCK, (blk + 1) * FOX_BLOCK
        qb = q[:, :, start:end].astype(jnp.float32)
        kb = k[:, :, :end].astype(jnp.float32)
        vb = v[:, :, :end].astype(jnp.float32)
        scores = jnp.einsum('bhqd,bhkd->bhqk', qb, kb) * scale
        scores = scores + cum[:, :, start:end, None] - cum[:, :, None, :end]
        q_pos = start + jnp.arange(FOX_BLOCK)
        mask = jnp.arange(end)[None, :] <= q_pos[:, None]
        scores = jnp.where(mask, scores, -jnp.inf)
        probs = jax.nn.softmax(scores, axis=-1)
        outs.append(jnp.einsum('bhqk,bhkd->bhqd', probs, vb))
    return jnp.concatenate(outs, axis=2)

def mlstm_chunkwise(q, k, v, i_pre, log_f):
    b, h, seq, dk = q.shape
    dv = v.shape[-1]
    nc = seq // MLSTM_CHUNK
    k = k * (1.0 / math.sqrt(dk))

    def chunks(t):
        return jnp.moveaxis(t.reshape(t.shape[:2] + (nc, MLSTM_CHUNK) + t.shape[3:]), 2, 0)

    qs, ks, vs = (chunks(t.astype(jnp.float32)) for t in (q, k, v))
    is_, fs = chunks(i_pre), chunks(log_f)
    causal = jnp.tril(jnp.ones((MLSTM_CHUNK, MLSTM_CHUNK), dtype=bool))

    def step(carry, inp):
        c_s, n_s, m = carry
        qc, kc, vc, ic, fc = inp
        bcum = jnp.cumsum(fc, axis=-1)
        dmat = bcum[..., :, None] - bcum[..., None, :] + ic[..., None, :]
        dmat = jnp.where(causal, dmat, -jnp.inf)
        inter = bcum + m[..., None]
        m_t = jnp.maximum(inter, jnp.max(dmat, axis=-1))
        w_inter = jnp.exp(inter - m_t)
        s = jnp.einsum('bhtd,bhsd->bhts', qc, kc) * jnp.exp(dmat - m_t[..., None])
        num = (w_inter[..., None] * jnp.einsum('bhtd,bhde->bhte', qc, c_s)
               + jnp.einsum('bhts,bhse->bhte', s, vc))
        den = w_inter * jnp.einsum('bhtd,bhd->bht', qc, n_s) + jnp.sum(s, axis=-1)
        h_out = num / jnp.maximum(jnp.abs(den), jnp.exp(-m_t))[..., None]
        b_last = bcum[..., -1]
        g = b_last[..., None] - bcum + ic
        m_new = jnp.maximum(b_last + m, jnp.max(g, axis=-1))
        decay = jnp.exp(b_last + m - m_new)
        wk = jnp.exp(g - m_new[..., None])
        c_new = decay[..., None, None] * c_s + jnp.einsum('bhs,bhsd,bhse->bhde', wk, kc, vc)
        n_new = decay[..., None] * n_s + jnp.einsum('bhs,bhsd->bhd', wk, kc)
        return (c_new, n_new, m_new), h_out

    init = (jnp.zeros((b, h, dk, dv), jnp.float32), jnp.zeros((b, h, dk), jnp.float32),
            jnp.zeros((b, h), jnp.float32))
    _, hs = lax.scan(step, init, (qs, ks, vs, is_, fs))
    return jnp.moveaxis(hs, 0, 2).reshape(b, h, seq, dv)

def moe_ffn(h, router_w, router_b, w_gu, b_gu, w_down, b_down):
    bsz, seq, d = h.shape
    n_tok = bsz * seq
    hf = h.reshape(n_tok, d)
    logits = (hf @ router_w).astype(jnp.float32) + router_b.astype(jnp.float32)
    top_v, top_i = lax.top_k(logits, TOP_K)
    gates = jax.nn.softmax(top_v, axis=-1)

    n_slot = n_tok * TOP_K
    buf_len = -(-n_slot // MOE_BLOCK) * MOE_BLOCK + N_EXPERTS * MOE_BLOCK
    n_blocks = buf_len // MOE_BLOCK
    e_flat = top_i.reshape(-1)
    tok_flat = jnp.arange(n_slot, dtype=jnp.int32) // TOP_K
    order = jnp.argsort(e_flat)
    e_sorted, tok_sorted, w_sorted = e_flat[order], tok_flat[order], gates.reshape(-1)[order]
    counts = jnp.bincount(e_flat, length=N_EXPERTS)
    starts = jnp.cumsum(counts) - counts
    padded = ((counts + MOE_BLOCK - 1) // MOE_BLOCK) * MOE_BLOCK
    pad_end = jnp.cumsum(padded)
    pad_start = pad_end - padded
    pos = pad_start[e_sorted] + (jnp.arange(n_slot) - starts[e_sorted])
    buf_tok = jnp.zeros((buf_len,), jnp.int32).at[pos].set(tok_sorted)
    buf_w = jnp.zeros((buf_len,), jnp.float32).at[pos].set(w_sorted)
    block_e = jnp.minimum(
        jnp.searchsorted(pad_end, jnp.arange(n_blocks) * MOE_BLOCK, side='right'), N_EXPERTS - 1)

    def expert_block(args):
        idx, e = args
        xb = hf[idx]
        gu = xb @ w_gu[e] + b_gu[e]
        gate = jnp.minimum(gu[:, :D_EXPERT], SWIGLU_LIMIT)
        up = jnp.clip(gu[:, D_EXPERT:], -SWIGLU_LIMIT, SWIGLU_LIMIT)
        act = (up + 1.0) * (gate * jax.nn.sigmoid(SWIGLU_ALPHA * gate))
        return act @ w_down[e] + b_down[e]

    y = lax.map(expert_block, (buf_tok.reshape(n_blocks, MOE_BLOCK), block_e))
    y = y.reshape(buf_len, d).astype(jnp.float32) * buf_w[:, None]
    out = jnp.zeros((n_tok, d), jnp.float32).at[buf_tok].add(y)
    return out.reshape(bsz, seq, d).astype(h.dtype)

def setup_inputs(seed: int = 0) -> dict:
    key = jax.random.key(seed)
    ks = jax.random.split(key, 20)
    n = jax.random.normal
    L = DEPTH
    return {
        "x": n(ks[0], (BATCH, SEQ, D_MODEL), jnp.float32),
        "attn_norm_w": 1.0 + 0.02 * n(ks[1], (L, D_MODEL), jnp.float32),
        "w_in": n(ks[2], (L, D_MODEL, IN_PROJ_WIDTH), jnp.float32) * D_MODEL ** -0.5,
        "fox_f_bias": 3.0 + 0.5 * n(ks[3], (L, FOX_HEADS), jnp.float32),
        "fox_q_norm_w": 1.0 + 0.02 * n(ks[4], (L, HEAD_DIM), jnp.float32),
        "fox_k_norm_w": 1.0 + 0.02 * n(ks[5], (L, HEAD_DIM), jnp.float32),
        "fox_out_norm_w": 1.0 + 0.02 * n(ks[6], (L, FOX_WIDTH), jnp.float32),
        "mlstm_conv_w": 0.5 * n(ks[7], (L, CONV_WIDTH, 2 * MLSTM_QK_WIDTH), jnp.float32),
        "mlstm_i_bias": 0.1 * n(ks[8], (L, MLSTM_HEADS), jnp.float32),
        "mlstm_f_bias": 3.0 + 0.5 * n(ks[9], (L, MLSTM_HEADS), jnp.float32),
        "mlstm_out_norm_w": 1.0 + 0.02 * n(ks[10], (L, MLSTM_V_WIDTH), jnp.float32),
        "w_out": n(ks[11], (L, MIX_WIDTH, D_MODEL), jnp.float32) * MIX_WIDTH ** -0.5,
        "moe_norm_w": 1.0 + 0.02 * n(ks[12], (L, D_MODEL), jnp.float32),
        "router_w": n(ks[13], (L, D_MODEL, N_EXPERTS), jnp.float32) * D_MODEL ** -0.5,
        "router_b": 0.01 * n(ks[14], (L, N_EXPERTS), jnp.float32),
        "expert_w_gate_up": n(ks[15], (L, N_EXPERTS, D_MODEL, 2 * D_EXPERT), jnp.float32) * D_MODEL ** -0.5,
        "expert_b_gate_up": 0.01 * n(ks[16], (L, N_EXPERTS, 2 * D_EXPERT), jnp.float32),
        "expert_w_down": n(ks[17], (L, N_EXPERTS, D_EXPERT, D_MODEL), jnp.float32) * D_EXPERT ** -0.5,
        "expert_b_down": 0.01 * n(ks[18], (L, N_EXPERTS, D_MODEL), jnp.float32),
    }

def reference(x, attn_norm_w, w_in, fox_f_bias, fox_q_norm_w, fox_k_norm_w, fox_out_norm_w,
              mlstm_conv_w, mlstm_i_bias, mlstm_f_bias, mlstm_out_norm_w, w_out, moe_norm_w,
              router_w, router_b, expert_w_gate_up, expert_b_gate_up, expert_w_down,
              expert_b_down):
    split_at = [int(s) for s in np.cumsum(SPLIT_WIDTHS)[:-1]]
    for layer in range(DEPTH):
        h = rms_norm(x, attn_norm_w[layer])
        proj = h @ w_in[layer]
        (fq, fk, fv, ff, mq, mk, mv, mi, mf, mo) = jnp.split(proj, split_at, axis=-1)

        fq = rms_norm(to_heads(fq, FOX_HEADS), fox_q_norm_w[layer])
        fk = rms_norm(to_heads(fk, FOX_HEADS), fox_k_norm_w[layer])
        fv = to_heads(fv, FOX_HEADS)
        fox_log_f = jax.nn.log_sigmoid(
            (ff + fox_f_bias[layer]).astype(jnp.float32)).transpose(0, 2, 1)
        fox_y = head_group_norm(forgetting_attention(fq, fk, fv, fox_log_f),
                                fox_out_norm_w[layer])

        qk = jax.nn.silu(causal_depthwise_conv(jnp.concatenate([mq, mk], axis=-1),
                                               mlstm_conv_w[layer]))
        mq, mk = qk[..., :MLSTM_QK_WIDTH], qk[..., MLSTM_QK_WIDTH:]
        m_i = (mi + mlstm_i_bias[layer]).astype(jnp.float32).transpose(0, 2, 1)
        m_log_f = jax.nn.log_sigmoid(
            (mf + mlstm_f_bias[layer]).astype(jnp.float32)).transpose(0, 2, 1)
        m_h = mlstm_chunkwise(to_heads(mq, MLSTM_HEADS), to_heads(mk, MLSTM_HEADS),
                              to_heads(mv, MLSTM_HEADS), m_i, m_log_f)
        mlstm_y = head_group_norm(m_h, mlstm_out_norm_w[layer]) * jax.nn.sigmoid(
            mo.astype(jnp.float32))

        mixed = jnp.concatenate([fox_y, mlstm_y], axis=-1).astype(x.dtype)
        x = x + mixed @ w_out[layer]

        h2 = rms_norm(x, moe_norm_w[layer])
        x = x + moe_ffn(h2, router_w[layer], router_b[layer], expert_w_gate_up[layer],
                        expert_b_gate_up[layer], expert_w_down[layer], expert_b_down[layer])
    return x


_drawn_inputs = setup_inputs


def setup_inputs(seed=0):
    import zlib

    import numpy as np

    out = dict(_drawn_inputs(seed))
    spreads = {}
    factors = {'mlstm_i_bias': 8.0, 'expert_b_gate_up': 8.0, 'expert_b_down': 8.0}
    for name, (base, spread) in spreads.items():
        noise = np.random.default_rng([zlib.crc32(name.encode()), seed]).standard_normal(out[name].shape)
        drawn = base * np.exp(spread * noise) if base else spread * noise
        out[name] = __import__('jax').numpy.asarray(drawn.astype(out[name].dtype))
    for name, factor in factors.items():
        out[name] = (out[name] * factor).astype(out[name].dtype)
    return out
```

```python
from contextlib import ExitStack
import concourse.bass as bass
from concourse import mybir

P = 128
D = 1024
S = 1024
TT = S // P
KT = D // P
H = 8
HD = 64
QK = 32
AUG = HD + 2
VA = HD + 1
NE = 32
TOPK = 4
CH = 512
W_IN = 3096
EPS = 1e-5
ALPHA = 1.702
LIMIT = 7.0
NEG = -1e30
SBMAX = S * TOPK // P + NE
SLOTS = SBMAX * P
NCH = 6
GU = 4
HC = CH // 2

C_FQ, C_FK, C_FV, C_FF, C_MQ, C_MV, C_MI, C_MF, C_MO = 0, 512, 1024, 1536, 1544, 2056, 2568, 2576, 2584


def layer_kernel(nc, A, out):
    f32, f32r, i32, u32 = mybir.dt.float32, mybir.dt.float32r, mybir.dt.int32, mybir.dt.uint32
    ALU, ACT, AX = mybir.AluOpType, mybir.ActivationFunctionType, mybir.AxisListType
    X = AX.X

    base = (nc.sbuf_base + 63) // 64 * 64
    KB = 1024
    A_X = base
    A_W = A_X + 64 * KB
    A_RAW = A_W + 64 * KB
    A_E = A_RAW + 48 * KB

    class Region:
        def __init__(self, at, size):
            self.at, self.end = at, at + size

        def take(self, name, shape, dt=f32):
            n = 4
            for d in shape[1:]:
                n *= d
            t = nc.alloc_sbuf_tensor_at(name, shape, dt, offset=self.at)
            self.at += (n + 63) // 64 * 64
            assert self.at <= self.end, name
            return t

    rx = Region(A_X, 64 * KB)
    XH = rx.take("XH", [P, KT, S], f32r)
    XL = rx.take("XL", [P, KT, S], f32r)
    rw = Region(A_W, 64 * KB)
    WH = rw.take("WH", [P, 2, KT, CH], f32r)
    WL = rw.take("WL", [P, 2, KT, CH], f32r)
    RAW = Region(A_RAW, 48 * KB).take("RAW", [P, 3, KT, CH])

    left = nc.sbuf_usable_end - A_E
    ext = Region(A_E, left)
    ident = ext.take("ident", [P, P])
    ones = ext.take("ones", [P, P])
    before = ext.take("before", [P, P])
    causal = ext.take("causal", [P, P])
    causalT = ext.take("causalT", [P, P])
    half = ext.take("half", [P, H])
    onec = ext.take("onec", [P, 1])
    rmsA = ext.take("rmsA", [P, TT])
    rmsB = ext.take("rmsB", [P, TT])
    TR = ext.take("TR", [P, TT, P])
    E0 = ext.at
    r1 = Region(E0, left - (E0 - A_E))
    xin = r1.take("xin", [P, 2, D])
    xn = r1.take("xn", [P, 2, D])
    r1b = Region(E0, 16 * KB + 256)
    zg = r1b.take("zg", [P, S])
    lf = r1b.take("lf", [P, S])
    cum = r1b.take("cum", [P, S])
    gt = r1b.take("gt", [P, S])
    SR = 3
    stage = r1.take("stage", [P, SR, H, AUG])
    gb = r1.take("gb", [P, 1])
    ssq = r1.take("ssq", [P, 2, H])
    rsq = r1.take("rsq", [P, 2, H])
    qkw = r1.take("qkw", [P, 2, HD])
    r1c = Region(A_RAW + 32 * KB, 16 * KB)
    wb1 = r1c.take("wb1", [P, D])
    GH = r1c.take("GH", [P, KT, P], f32r)
    GL = r1c.take("GL", [P, KT, P], f32r)
    R = r1c.take("R", [P, S])
    graw = Region(A_W + 48 * KB, 4 * KB).take("graw", [P, KT, P])
    sqr = Region(A_W + 52 * KB, 4 * KB).take("sqr", [P, D])
    sq = r1.take("sq", [P, CH])

    bank_pairs = [nc.alloc_psum_tensor(f"banks{2 * i}_{2 * i + 1}", [P, 2 * CH], f32) for i in range(4)]
    ps = [bank_pairs[i // 2][:, (i % 2) * CH:(i % 2 + 1) * CH] for i in range(8)]

    def pair(i, n):
        return bank_pairs[i][:, 0:n]

    def dram(name, shape, dt=f32):
        return nc.dram_tensor(name, shape, dt, kind="Internal").ap()
    dQ, dK = dram("dQ", [S, H * AUG]), dram("dK", [S, H * AUG])
    dV, dMV, dMO = dram("dV", [S, CH]), dram("dMV", [S, CH]), dram("dMO", [S, CH])
    dQK = dram("dQK", [4 * P, S])
    dX1, dH2 = dram("dX1", [S, D]), dram("dH2", [S, D])
    dTok = dram("dTok", [SLOTS, 1])
    dY = dram("dY", [SLOTS, D])
    dTab = dram("dTab", [SBMAX, 1], i32)
    dN = dram("dN", [1, 1], i32)

    x2 = A["x"].rearrange("b s d -> (b s) d")
    w_in = A["w_in"][0].rearrange("(k p) n -> p k n", p=P)
    w_out = A["w_out"][0].rearrange("(k p) n -> p k n", p=P)
    out2 = out.rearrange("b s d -> (b s) d")

    held = []

    def sem(name):
        held.append(nc.alloc_semaphore(name))
        return held[-1]

    def run(stage_):
        held.clear()
        stage_()
        nc.clear_and_free_semaphores(list(held))
        nc.all_engine_barrier(sem_only=True)

    def tok(t):
        return slice(t * P, (t + 1) * P)

    def bc(ap, shape):
        return ap.broadcast_to(shape)

    def mm3(pe, o, lh, ll, rh, rl, start, stop):
        pe.matmul(o, lh, rh, start=start, stop=False)
        pe.matmul(o, lh, rl, start=False, stop=False)
        return pe.matmul(o, ll, rh, start=False, stop=stop)

    def chain(eng, name):
        s, n = sem(name), [0]

        def link(ins):
            n[0] += 1
            ins.then_inc(s, 1)
            eng.wait_ge(s, n[0])
        return link

    def inv_root(pool, link, o, sums, n):
        link(pool.tensor_scalar(o, sums, 1.0 / n, EPS, ALU.mult, ALU.add))
        return pool.tensor_tensor(o, o, half[:, 0:o.shape[1]], ALU.pow)

    KINDS = ("q", "k", "v", "mv", "qk", "mo")
    COLS = (C_FQ, C_FK, C_FV, C_MV, C_MQ, C_MO)
    READER = {"q": "dve", "k": "dve", "v": "act", "mv": "act", "qk": "act", "mo": "act"}
    OUTS = [("g", 0), ("g", 1)] + [(k, j) for k in KINDS for j in range(TT)]
    RING = 6
    reads = {"dve": 0, "act": 0}
    FREED = []
    for kind, _ in OUTS:
        e = READER.get(kind, "dve")
        reads[e] += 1
        FREED.append((e, reads[e]))
    STAGED = [(k, j) for k in KINDS for j in range(TT)]
    UNITS = range(len(STAGED))

    def stage1():
        s_x = [sem("s1_x0"), sem("s1_x1")]
        s_c, s_zero, s_gw, s_qkw = sem("s1_const"), sem("s1_zero"), sem("s1_gatew"), sem("s1_qkw")
        s_wb = sem("s1_wb")
        s_ss, s_rstd, s_xn, s_tp, s_hi, s_hT = (sem("s1_" + n) for n in ("ss", "rstd", "xn", "tp", "hi", "hT"))
        s_ghi, s_g = sem("s1_ghi"), sem("s1_g")
        s_raw = [sem("s1_raw0"), sem("s1_raw1")]
        s_whi, s_w, s_wused = sem("s1_whi"), sem("s1_w"), sem("s1_wused")
        s_out = sem("s1_out")
        s_free = {"dve": sem("s1_freed_dve"), "act": sem("s1_freed_act")}
        s_sq, s_ssq, s_rsq = sem("s1_sq"), sem("s1_ssq"), sem("s1_rsq")
        s_scaled, s_staged, s_sent = sem("s1_scaled"), sem("s1_staged"), [sem(f"s1_sent{i}") for i in range(SR)]
        s_zg, s_e, s_ln, s_tr, s_R, s_aug = (sem("s1_" + n) for n in ("zg", "e", "ln", "tr", "R", "aug"))

        def staged_wait(eng, u):
            if u >= SR:
                eng.wait_ge(s_sent[u % SR], 16 * (u // SR))

        with nc.Block() as block:
            @block.sync
            def _(sp):
                sp.dma_start(wb1[:], A["attn_norm_w"][0].partition_broadcast(P)).then_inc(s_wb, 16)
                for t in range(TT):
                    if t >= 2:
                        sp.wait_ge(s_xn, t - 1)
                    sp.dma_start(xin[:, t % 2, :], x2[tok(t), :]).then_inc(s_x[t % 2], 16)
                    if t == 1:
                        sp.wait_ge(s_zero, 1)
                        for r, c in ((0, C_FF), (32, C_MI), (64, C_MF)):
                            sp.dma_start(graw[:, :, r:r + H], w_in[:, :, c:c + H]).then_inc(s_gw, 16)
                        for r, n in ((0, "fox_f_bias"), (32, "mlstm_i_bias"), (64, "mlstm_f_bias")):
                            sp.dma_start(gb[r:r + H, :], A[n].rearrange("a h -> h a")).then_inc(s_gw, 16)
                        sp.dma_start(qkw[:, 0, :], A["fox_q_norm_w"][0].partition_broadcast(P)).then_inc(s_qkw, 16)
                        sp.dma_start(qkw[:, 1, :], A["fox_k_norm_w"][0].partition_broadcast(P)).then_inc(s_qkw, 16)
                        for n in (0, 1):
                            sp.dma_start(RAW[:, n], w_in[:, :, COLS[n]:COLS[n] + CH]).then_inc(s_raw[n], 16)
                for u in UNITS:
                    kind, j = STAGED[u]
                    n = u // TT
                    if j == 0 and 2 <= n + 1 < len(KINDS):
                        sp.wait_ge(s_w, n)
                        sp.dma_start(RAW[:, (n + 1) % 2], w_in[:, :, COLS[n + 1]:COLS[n + 1] + CH]).then_inc(s_raw[(n + 1) % 2], 16)
                    src = stage[:, u % SR].rearrange("p h c -> p (h c)")
                    if kind in ("q", "k"):
                        sp.wait_ge(s_scaled, u + 1)
                        sp.dma_start((dQ if kind == "q" else dK)[tok(j), :], src).then_inc(s_sent[u % SR], 16)
                    else:
                        sp.wait_ge(s_staged, u - 2 * TT + 1)
                        to = {"v": dV, "mv": dMV, "mo": dMO}
                        dst = to[kind][tok(j), :] if kind in to else dQK[tok(j // 2), (j % 2) * CH:(j % 2 + 1) * CH]
                        sp.dma_start(dst, src[:, 0:CH]).then_inc(s_sent[u % SR], 16)
                for i in range(SR):
                    sp.wait_ge(s_sent[i], 16 * len([u for u in UNITS if u % SR == i]))

            @block.gpsimd
            def _(pool):
                link = chain(pool, "s1_pool")
                pool.memset(graw[:], 0.0)
                pool.memset(gb[:], 0.0).then_inc(s_zero, 1)
                pool.memset(half[:], -0.5)
                pool.memset(onec[:], 1.0)
                pool.memset(ones[:], 1.0)
                pool.memset(before[:], 1.0)
                pool.memset(causal[:], 0.0)
                pool.memset(causalT[:], 0.0)
                pool.memset(ident[:], 0.0).then_inc(s_c, 1)
                pool.wait_ge(s_c, 1)
                pool.affine_select(out=ident[:], in_=ident[:], compare_op=ALU.not_equal, fill=1.0,
                                   base=0, pattern=[[-1, P]], channel_multiplier=1)
                pool.affine_select(out=before[:], in_=before[:], compare_op=ALU.is_gt, fill=0.0,
                                   base=0, pattern=[[1, P]], channel_multiplier=-1)
                pool.affine_select(out=causal[:], in_=causal[:], compare_op=ALU.is_ge, fill=NEG,
                                   base=0, pattern=[[-1, P]], channel_multiplier=1)
                pool.affine_select(out=causalT[:], in_=causalT[:], compare_op=ALU.is_ge, fill=NEG,
                                   base=0, pattern=[[1, P]], channel_multiplier=-1).then_inc(s_c, 1)
                for t in range(TT):
                    pool.wait_ge(s_ss, t + 1)
                    r = rmsA[:, t:t + 1]
                    inv_root(pool, link, r, r, D).then_inc(s_rstd, 1)
                pool.wait_ge(s_qkw, 32)
                pool.tensor_scalar(qkw[:, 0, :], qkw[:, 0, :], HD ** -0.5, None, ALU.mult).then_inc(s_c, 1)
                pool.wait_ge(s_c, 3)
                for u in range(2 * TT):
                    pool.wait_ge(s_ssq, u + 1)
                    if u >= 2:
                        pool.wait_ge(s_free["dve"], FREED[u][1])
                    inv_root(pool, link, rsq[:, u % 2], ssq[:, u % 2], HD).then_inc(s_rsq, 1)
                    pool.wait_ge(s_aug, u + 1)
                    v = stage[:, u % SR, :, 0:HD]
                    w = bc(qkw[:, u // TT, :].unsqueeze(1), [P, H, HD])
                    pool.tensor_tensor(v, v, w, ALU.mult).then_inc(s_scaled, 1)

            @block.scalar
            def _(act):
                link = chain(act, "s1_act")

                def split_hi(n):
                    act.wait_ge(s_raw[n % 2], 16 * (n // 2 + 1))
                    if n >= 2:
                        act.wait_ge(s_wused, n - 1)
                    act.activation(WH[:, n % 2], RAW[:, n % 2], ACT.Copy).then_inc(s_whi, 1)

                act.wait_ge(s_c, 2)
                for t in range(TT):
                    act.wait_ge(s_x[t % 2], 16 * (t // 2 + 1))
                    if t >= 1:
                        act.wait_ge(s_ss, t)
                    act.activation(sqr[:], xin[:, t % 2], ACT.Square, accum_out=rmsA[:, t:t + 1]).then_inc(s_ss, 1)
                    if t >= 1:
                        hi_of(act, t - 1, s_tp, s_hi, XH)
                hi_of(act, TT - 1, s_tp, s_hi, XH)
                act.wait_ge(s_gw, 96)
                act.activation(GH[:], graw[:], ACT.Copy).then_inc(s_ghi, 1)
                split_hi(0)
                split_hi(1)
                act.wait_ge(s_zg, 2)
                link(act.activation(lf[:], zg[:], ACT.Abs))
                link(act.activation(lf[:], lf[:], ACT.Exp, scale=-1.0))
                act.activation(lf[:], lf[:], ACT.Ln, bias=onec[:, 0:1]).then_inc(s_ln, 1)
                for b in range(2):
                    act.wait_ge(s_tr, b + 1)
                    act.activation(TR[:, 4 * b:4 * b + 4, :].rearrange("p t c -> p (t c)"), ps[b][:], ACT.Copy).then_inc(s_e, 1)
                for u in UNITS:
                    kind, j = STAGED[u]
                    n, o = u // TT, u + 2
                    b = ps[2 + o % RING]
                    if j == 2 and 1 <= n < len(KINDS) - 1:
                        split_hi(n + 1)
                    act.wait_ge(s_out, o + 1)
                    if kind in ("q", "k"):
                        if u >= 1:
                            act.wait_ge(s_ssq, u)
                        act.activation(sq[:], b[:], ACT.Square).then_inc(s_sq, 1)
                    else:
                        staged_wait(act, u)
                        fn = ACT.Sigmoid if kind == "mo" else ACT.Copy
                        dst = stage[:, u % SR].rearrange("p h c -> p (h c)")[:, 0:CH]
                        ins = act.activation(dst, b[:], fn)
                        ins.then_inc(s_free["act"], 1)
                        act.wait_ge(s_free["act"], FREED[o][1])
                        act.sem_inc(s_staged, 1)

            @block.vector
            def _(dve):
                link = chain(dve, "s1_dve")

                def split_lo(n):
                    dve.wait_ge(s_whi, n + 1)
                    dve.tensor_tensor(WL[:, n % 2], RAW[:, n % 2], WH[:, n % 2].bitcast(f32), ALU.subtract).then_inc(s_w, 1)

                dve.wait_ge(s_wb, 16)
                for t in range(TT):
                    dve.wait_ge(s_rstd, t + 1)
                    if t >= 2:
                        dve.wait_ge(s_tp, t - 1)
                    dve.scalar_tensor_tensor(out=xn[:, t % 2], in0=xin[:, t % 2], scalar=rmsA[:, t:t + 1], in1=wb1[:],
                                             op0=ALU.mult, op1=ALU.mult).then_inc(s_xn, 1)
                    if t >= 1:
                        lo_of(dve, t - 1, s_hi, s_hT, XH, XL)
                lo_of(dve, TT - 1, s_hi, s_hT, XH, XL)
                dve.wait_ge(s_ghi, 1)
                dve.tensor_tensor(GL[:], graw[:], GH[:].bitcast(f32), ALU.subtract).then_inc(s_g, 1)
                split_lo(0)
                dve.wait_ge(s_g, 1)
                split_lo(1)
                for o in (0, 1):
                    dve.wait_ge(s_out, o + 1)
                    if o == 0:
                        dve.wait_ge(s_hT, TT)
                    dve.tensor_scalar(zg[:, o * CH:(o + 1) * CH], ps[2 + o][:], gb[:, 0:1], None, ALU.add).then_inc(s_zg, 1)
                    dve.wait_ge(s_zg, o + 1)
                    dve.sem_inc(s_free["dve"], 1)
                dve.wait_ge(s_ln, 1)
                link(dve.scalar_tensor_tensor(out=lf[:], in0=zg[:], scalar=0.0, in1=lf[:], op0=ALU.min, op1=ALU.subtract))
                link(dve.memset(gt[:], 1.0))
                link(dve.tensor_tensor_scan(cum[:], gt[:], lf[:], 0.0, ALU.mult, ALU.add))
                link(dve.memset(R[:], 0.0))
                link(dve.tensor_copy(R[0:H], cum[0:H]))
                link(dve.tensor_copy(gt[32:32 + H], cum[64:64 + H]))
                link(dve.tensor_tensor(R[32:32 + H], zg[32:32 + H], gt[32:32 + H], ALU.subtract))
                link(dve.tensor_tensor_scan(gt[32:32 + H], R[32:32 + H], R[32:32 + H], 0.0, ALU.max, ALU.max))
                link(dve.tensor_copy(R[64:64 + H], gt[32:32 + H]))
                link(dve.tensor_tensor(gt[64:64 + H], R[64:64 + H], cum[64:64 + H], ALU.add))
                link(dve.tensor_copy(R[96:96 + H], gt[64:64 + H]))
                dve.sem_inc(s_R, 1)
                dve.wait_ge(s_e, 2)
                for u in UNITS:
                    kind, j = STAGED[u]
                    n, o = u // TT, u + 2
                    b = ps[2 + o % RING]
                    if j == 2 and 1 <= n < len(KINDS) - 1:
                        split_lo(n + 1)
                    if kind not in ("q", "k"):
                        continue
                    dve.wait_ge(s_sq, u + 1)
                    if u >= 2:
                        dve.wait_ge(s_rsq, u - 1)
                    dve.tensor_reduce(ssq[:, u % 2], sq[:].rearrange("p (h c) -> p h c", h=H), X, ALU.add).then_inc(s_ssq, 1)
                    staged_wait(dve, u)
                    a, c = (HD, HD + 1) if kind == "q" else (HD + 1, HD)
                    dve.tensor_scalar(stage[:, u % SR, :, a:a + 1], TR[:, j, 0:H].unsqueeze(2), 1.0 if kind == "q" else -1.0, None, ALU.mult)
                    dve.memset(stage[:, u % SR, :, c:c + 1], 1.0)
                    dve.wait_ge(s_rsq, u + 1)
                    r = bc(rsq[:, u % 2].unsqueeze(2), [P, H, HD])
                    dve.tensor_tensor(stage[:, u % SR, :, 0:HD], b[:].rearrange("p (h c) -> p h c", h=H), r, ALU.mult).then_inc(s_free["dve"], 1)
                    dve.wait_ge(s_free["dve"], FREED[o][1])
                    dve.sem_inc(s_aug, 1)

            @block.tensor
            def _(pe):
                pe.wait_ge(s_c, 2)
                for t in range(TT):
                    pe.wait_ge(s_xn, t + 1)
                    transposes_of(pe, t, xn[:, t % 2], s_hT, s_tp)
                pe.wait_ge(s_hT, TT)
                pe.wait_ge(s_g, 1)
                for hf in range(2):
                    cols = slice(hf * CH, (hf + 1) * CH)
                    for k in range(KT):
                        last = mm3(pe, ps[2 + hf][:], GH[:, k], GL[:, k], XH[:, k, cols], XL[:, k, cols], k == 0, k == KT - 1)
                    last.then_inc(s_out, 1)
                for u in UNITS:
                    kind, j = STAGED[u]
                    n, o = u // TT, u + 2
                    if u == 2:
                        pe.wait_ge(s_R, 1)
                        for b in range(2):
                            for i in range(4):
                                last = pe.transpose(ps[b][:, i * P:(i + 1) * P], R[:, tok(4 * b + i)], ident[:])
                            last.then_inc(s_tr, 1)
                    if j == 0:
                        pe.wait_ge(s_w, n + 1)
                    if o >= RING:
                        e, c = FREED[o - RING]
                        pe.wait_ge(s_free[e], c)
                    b = ps[2 + o % RING]
                    for k in range(KT):
                        if kind == "qk":
                            c, cols = tok(j // 2), slice((j % 2) * CH, (j % 2 + 1) * CH)
                            last = mm3(pe, b[:], WH[:, n % 2, k, c], WL[:, n % 2, k, c], XH[:, k, cols], XL[:, k, cols], k == 0, k == KT - 1)
                        else:
                            last = mm3(pe, b[:], XH[:, k, tok(j)], XL[:, k, tok(j)], WH[:, n % 2, k], WL[:, n % 2, k], k == 0, k == KT - 1)
                    last.then_inc(s_out, 1)
                    if j == TT - 1:
                        pe.wait_ge(s_out, o + 1)
                        pe.sem_inc(s_wused, 1)

    def transposes_of(pe, t, src, s_free, s_done):
        if t >= 2:
            pe.wait_ge(s_free, t - 1)
        for g in range(2):
            b = ps[2 * (t % 2) + g]
            for i in range(4):
                last = pe.transpose(b[:, i * P:(i + 1) * P], src[:, (4 * g + i) * P:(4 * g + i + 1) * P], ident[:])
        last.then_inc(s_done, 1)

    def hi_of(act, t, s_done, s_hi, to):
        act.wait_ge(s_done, t + 1)
        for g in range(2):
            ins = act.activation(to[:, 4 * g:4 * g + 4, tok(t)], ps[2 * (t % 2) + g][:].rearrange("p (k c) -> p k c", k=4), ACT.Copy)
        ins.then_inc(s_hi, 1)

    def lo_of(dve, t, s_hi, s_done, hi, lo):
        dve.wait_ge(s_hi, t + 1)
        for g in range(2):
            ins = dve.tensor_tensor(lo[:, 4 * g:4 * g + 4, tok(t)], ps[2 * (t % 2) + g][:].rearrange("p (k c) -> p k c", k=4),
                                    hi[:, 4 * g:4 * g + 4, tok(t)].bitcast(f32), ALU.subtract)
        ins.then_inc(s_done, 1)

    r2 = Region(A_X, 128 * KB)
    U = r2.take("U", [P, 4, S + 3])
    CV = r2.take("CV", [P, 4, S])
    SG = r2.take("SG", [P, 4, S])
    QKT = r2.take("QKT", [P, 4, S])
    VAU = r2.take("VAU", [P, TT, H, VA])
    KTOK = r2.take("KTOK", [P, TT, 2 * P])
    SELA = r2.take("SELA", [P, H, P])
    SELM = r2.take("SELM", [P, H, P])
    last_row = r2.take("last_row", [P, P])
    QZ = r2.take("QZ", [P, 2, H, P])
    r2r = Region(A_RAW, 32 * KB)
    MY = r2r.take("MY", [P, TT, CH])
    MOS = r2r.take("MOS", [P, 2, CH])
    mow = r2r.take("mow", [P, CH])
    WT = r2r.take("WT", [P, H, P])
    CST = r2r.take("CST", [P, 2, 4 * VA])
    kw = r2r.take("kw", [P, 2 * P])
    r2e = Region(E0, left - (E0 - A_E))
    PT = r2e.take("PT", [P, H, P])
    num = r2e.take("num", [P, H, VA])
    tmp = r2e.take("tmp", [P, H, VA])
    yh = r2e.take("yh", [P, 2, H, HD])
    ysq = r2e.take("ysq", [P, CH])
    MB = r2e.take("MB", [P, TT + 1, H])
    ex = r2e.take("ex", [P, 4, TT, H])
    cw = r2e.take("cw", [P, 4, 4])
    den = r2e.take("den", [P, 2, H])
    ysum = r2e.take("ysum", [P, 2, H])

    def stage2():
        def s2(n):
            return sem("s2_" + n)
        s_u, s_cw, s_v, s_w, s_mo = s2("u"), s2("convw"), s2("values"), s2("outw"), [s2("mo0"), s2("mo1")]
        s_qzero, s_qz, s_uz, s_sel, s_vone = s2("qzero"), s2("qz"), s2("uz"), s2("sel"), s2("vone")
        s_cv, s_sg, s_qk, s_kt, s_ktok = s2("conv"), s2("sig"), s2("qkt"), s2("kt"), s2("ktok")
        s_mb, s_mbs, s_exin, s_ex = s2("mb"), s2("mbs"), s2("exin"), s2("ex")
        s_D, s_S, s_int, s_Dm, s_WT, s_PT = s2("D"), s2("S"), s2("inter"), s2("Dmasked"), s2("WT"), s2("PT")
        s_tmp, s_kw, s_intra, s_num, s_upd, s_C = s2("tmp"), s2("kw"), s2("intra"), s2("num"), s2("upd"), s2("C")
        s_y, s_ysq, s_ysum, s_rs, s_done, s_mow = s2("y"), s2("ysq"), s2("ysum"), s2("rs"), s2("done"), s2("mow")

        with nc.Block() as block:
            @block.sync
            def _(sp):
                for j in range(4):
                    sp.dma_start(cw[:, j], A["mlstm_conv_w"][0, j].rearrange("(c p) -> p c", p=P), allow_slow_non_contiguous=True).then_inc(s_cw, 16)
                sp.dma_start(U[:, :, 3:S + 3], dQK.rearrange("(c p) s -> p c s", p=P)).then_inc(s_u, 16)
                sp.dma_start(mow[:], A["mlstm_out_norm_w"][0].partition_broadcast(P)).then_inc(s_w, 16)
                for t in range(TT):
                    sp.dma_start(VAU[:, t, :, 0:HD], dMV[tok(t), :].rearrange("p (h d) -> p h d", h=H)).then_inc(s_v, 16)
                for t in range(TT):
                    if t >= 2:
                        sp.wait_ge(s_mow, t - 1)
                    sp.dma_start(MOS[:, t % 2], dMO[tok(t), :]).then_inc(s_mo[t % 2], 16)

            @block.gpsimd
            def _(pool):
                link = chain(pool, "s2_pool")
                pool.memset(U[:, :, 0:3], 0.0).then_inc(s_uz, 1)
                pool.memset(SELA[:], 0.0)
                pool.memset(SELM[:], 0.0)
                link(pool.memset(last_row[:], 0.0))
                pool.memset(CST[:], 0.0)
                pool.affine_select(out=last_row[:], in_=last_row[:], compare_op=ALU.not_equal, fill=1.0,
                                   base=1 - P, pattern=[[0, P]], channel_multiplier=1).then_inc(s_sel, 1)
                pool.affine_select(out=SELA[:], in_=SELA[:], compare_op=ALU.not_equal, fill=1.0,
                                   base=-32, pattern=[[-1, H], [0, P]], channel_multiplier=1)
                pool.affine_select(out=SELM[:], in_=SELM[:], compare_op=ALU.not_equal, fill=-1.0,
                                   base=-64, pattern=[[-1, H], [0, P]], channel_multiplier=1).then_inc(s_sel, 1)
                pool.memset(VAU[:, :, :, HD:VA], 1.0).then_inc(s_vone, 1)
                pool.memset(QZ[:], 0.0).then_inc(s_qzero, 1)
                pool.wait_ge(s_ktok, 4)
                pool.wait_ge(s_ex, 1)
                pool.wait_ge(s_w, 16)

                def finish(t):
                    pool.wait_ge(s_mo[t % 2], 16 * (t // 2 + 1))
                    pool.tensor_tensor(MOS[:, t % 2], MOS[:, t % 2], mow[:], ALU.mult).then_inc(s_rs, 1)
                    pool.wait_ge(s_ysum, t + 1)
                    link(inv_root(pool, link, ysum[:, t % 2], ysum[:, t % 2], HD))
                    pool.wait_ge(s_ysq, t + 1)
                    pool.wait_ge(s_rs, t + 1)
                    y = yh[:, t % 2]
                    link(pool.tensor_tensor(y, y, bc(ysum[:, t % 2].unsqueeze(2), [P, H, HD]), ALU.mult))
                    pool.tensor_tensor(MY[:, t], y.rearrange("p h d -> p (h d)"), MOS[:, t % 2], ALU.mult).then_inc(s_mow, 1)

                for t in range(TT):
                    if t >= 1:
                        pool.wait_ge(s_upd, t)
                    k = kw[:].rearrange("p (h d) -> p h d", h=H)
                    pool.tensor_tensor(k, KTOK[:, t].rearrange("p (h d) -> p h d", h=H),
                                       bc(ex[:, 1, t].unsqueeze(2), [P, H, QK]), ALU.mult).then_inc(s_kw, 1)
                    if t >= 1:
                        finish(t - 1)
                finish(TT - 1)

            @block.scalar
            def _(act):
                for c in range(4):
                    act.wait_ge(s_cv, c + 1)
                    act.activation(SG[:, c], CV[:, c], ACT.Sigmoid).then_inc(s_sg, 1)
                def spread(t):
                    if t >= 2:
                        act.wait_ge(s_S, t - 1)
                    for h in range(H):
                        rows = slice(32 * (h % 4), 32 * (h % 4) + 32)
                        last = act.activation(QZ[rows, t % 2, h], QKT[rows, h // 4, tok(t)], ACT.Copy)
                    last.then_inc(s_qz, 1)

                act.wait_ge(s_qk, 2)
                act.wait_ge(s_qzero, 1)
                spread(0)
                for i in range(4):
                    act.wait_ge(s_kt, i + 1)
                    act.activation(KTOK[:, 4 * (i % 2):4 * (i % 2) + 4, (i // 2) * P:(i // 2 + 1) * P],
                                   ps[4 + i][:].rearrange("p (t c) -> p t c", t=4), ACT.Copy).then_inc(s_ktok, 1)
                act.wait_ge(s_exin, 1)
                act.activation(ex[:], ex[:], ACT.Exp).then_inc(s_ex, 1)
                for t in range(TT + 1):
                    if t < TT:
                        act.wait_ge(s_Dm, t + 1)
                        act.activation(WT[:], WT[:], ACT.Exp).then_inc(s_WT, 1)
                        if t + 1 < TT:
                            spread(t + 1)
                    if t >= 1:
                        act.wait_ge(s_y, t)
                        if t >= 2:
                            act.wait_ge(s_ysum, t - 1)
                        act.activation(ysq[:], yh[:, (t - 1) % 2].rearrange("p h d -> p (h d)"), ACT.Square).then_inc(s_ysq, 1)

            @block.vector
            def _(dve):
                link = chain(dve, "s2_dve")
                dve.wait_ge(s_cw, 64)
                dve.wait_ge(s_u, 16)
                dve.wait_ge(s_uz, 1)
                for c in range(4):
                    link(dve.tensor_scalar(CV[:, c], U[:, c, 3:S + 3], cw[:, 3, c:c + 1], None, ALU.mult))
                    for j in (2, 1):
                        link(dve.scalar_tensor_tensor(out=CV[:, c], in0=U[:, c, j:j + S], scalar=cw[:, j, c:c + 1], in1=CV[:, c], op0=ALU.mult, op1=ALU.add))
                    dve.scalar_tensor_tensor(out=CV[:, c], in0=U[:, c, 0:S], scalar=cw[:, 0, c:c + 1], in1=CV[:, c],
                                             op0=ALU.mult, op1=ALU.add).then_inc(s_cv, 1)
                dve.wait_ge(s_mb, 1)
                dve.memset(MB[:, 0], 0.0)
                link(dve.tensor_copy(MB[:, 1:], ps[0][:, 0:TT * H].rearrange("p (t h) -> p t h", t=TT)))
                dve.tensor_tensor(ex[:, 0], MB[:, 0:TT], TR[:, :, 64:64 + H], ALU.subtract)
                dve.tensor_tensor(ex[:, 1], TR[:, :, 32:32 + H], MB[:, 1:], ALU.subtract)
                dve.tensor_tensor(ex[:, 2], MB[:, 0:TT], MB[:, 1:], ALU.subtract)
                dve.tensor_scalar(ex[:, 3], TR[:, :, 96:96 + H], -1.0, None, ALU.mult).then_inc(s_exin, 1)
                for c in range(4):
                    dve.wait_ge(s_sg, c + 1)
                    dve.scalar_tensor_tensor(out=QKT[:, c], in0=CV[:, c], scalar=1.0 if c < 2 else QK ** -0.5, in1=SG[:, c],
                                             op0=ALU.mult, op1=ALU.mult).then_inc(s_qk, 1)
                dve.wait_ge(s_ex, 1)

                def mask(t):
                    dve.wait_ge(s_D, t + 1)
                    if t >= 1:
                        dve.wait_ge(s_PT, t)
                    for g in range(2):
                        last = dve.scalar_tensor_tensor(out=WT[:, 4 * g:4 * g + 4], in0=ps[g][:].rearrange("p (h c) -> p h c", h=4), scalar=0.0,
                                                        in1=bc(causalT[:].unsqueeze(1), [P, 4, P]), op0=ALU.min, op1=ALU.add)
                    last.then_inc(s_Dm, 1)

                mask(0)
                for t in range(TT):
                    dve.wait_ge(s_S, t + 1)
                    dve.wait_ge(s_WT, t + 1)
                    if t >= 1:
                        dve.wait_ge(s_intra, t)
                    for g in range(2):
                        last = dve.tensor_tensor(PT[:, 4 * g:4 * g + 4], ps[2 + g][:].rearrange("p (h c) -> p h c", h=4), WT[:, 4 * g:4 * g + 4], ALU.mult)
                    last.then_inc(s_PT, 1)
                    dve.wait_ge(s_int, t + 1)
                    for g in range(2):
                        last = dve.tensor_tensor(tmp[:, 4 * g:4 * g + 4], ps[4 + g][:, 0:4 * VA].rearrange("p (h c) -> p h c", h=4),
                                                 bc(ex[:, 0, t, 4 * g:4 * g + 4].unsqueeze(2), [P, 4, VA]), ALU.mult)
                    last.then_inc(s_tmp, 1)
                    dve.wait_ge(s_tmp, t + 1)
                    dve.wait_ge(s_intra, t + 1)
                    for g in range(2):
                        last = dve.tensor_tensor(num[:, 4 * g:4 * g + 4], tmp[:, 4 * g:4 * g + 4], ps[6 + g][:, 0:4 * VA].rearrange("p (h c) -> p h c", h=4), ALU.add)
                    last.then_inc(s_num, 1)
                    if t + 1 < TT:
                        mask(t + 1)
                    dve.wait_ge(s_upd, t + 1)
                    for h in range(H):
                        j, g = h % 4, h // 4
                        rows, cols = slice(32 * j, 32 * j + 32), slice(j * VA, (j + 1) * VA)
                        last = dve.scalar_tensor_tensor(out=CST[rows, g, cols], in0=CST[rows, g, cols], scalar=ex[rows, 2, t, h:h + 1],
                                                        in1=ps[4 + g][rows, cols], op0=ALU.mult, op1=ALU.add)
                    last.then_inc(s_C, 1)
                    dve.wait_ge(s_num, t + 1)
                    d = den[:, t % 2]
                    link(dve.tensor_tensor(d.unsqueeze(2), num[:, :, HD:VA], ex[:, 3, t].unsqueeze(2), ALU.max))
                    link(dve.scalar_tensor_tensor(out=d.unsqueeze(2), in0=num[:, :, HD:VA], scalar=-1.0, in1=d.unsqueeze(2), op0=ALU.mult, op1=ALU.max))
                    link(dve.reciprocal(d, d))
                    if t >= 2:
                        dve.wait_ge(s_mow, t - 1)
                    dve.tensor_tensor(yh[:, t % 2], num[:, :, 0:HD], bc(d.unsqueeze(2), [P, H, HD]), ALU.mult).then_inc(s_y, 1)
                    dve.wait_ge(s_y, t + 1)
                    dve.wait_ge(s_ysq, t + 1)
                    dve.tensor_reduce(ysum[:, t % 2], ysq[:].rearrange("p (h c) -> p h c", h=H), X, ALU.add).then_inc(s_ysum, 1)
                    dve.wait_ge(s_C, t + 1)

            @block.tensor
            def _(pe):
                pe.wait_ge(s_sel, 1)
                pe.matmul(ps[0][:, 0:TT * H], last_row[:], TR[:, :, 64:64 + H], start=True, stop=True).then_inc(s_mb, 1)
                pe.wait_ge(s_qk, 4)
                for i in range(4):
                    c = 2 + i // 2
                    for n in range(4):
                        last = pe.transpose(ps[4 + i][:, n * P:(n + 1) * P], QKT[:, c, tok(4 * (i % 2) + n)], ident[:])
                    last.then_inc(s_kt, 1)
                pe.wait_ge(s_sel, 2)
                pe.wait_ge(s_exin, 1)

                def scores(t):
                    if t >= 1:
                        pe.wait_ge(s_Dm, t)
                    for h in range(H):
                        o = ps[h // 4][:, (h % 4) * P:(h % 4 + 1) * P]
                        pe.matmul(o, R[:, tok(t)], SELA[:, h], start=True, stop=False)
                        last = pe.matmul(o, SELM[:, h], R[:, tok(t)], start=False, stop=True)
                    last.then_inc(s_D, 1)
                    if t >= 1:
                        pe.wait_ge(s_PT, t)
                    pe.wait_ge(s_qz, t + 1)
                    for g in range(2):
                        last = pe.matmul(ps[2 + g][:], QKT[:, 2 + g, tok(t)], QZ[:, t % 2, 4 * g:4 * g + 4].rearrange("p h c -> p (h c)"), start=True, stop=True)
                    last.then_inc(s_S, 1)

                scores(0)
                pe.wait_ge(s_vone, 1)
                pe.wait_ge(s_v, 16 * TT)
                pe.wait_ge(s_ktok, 4)
                for t in range(TT):
                    if t >= 1:
                        pe.wait_ge(s_C, t)
                    for g in range(2):
                        last = pe.matmul(ps[4 + g][:, 0:4 * VA], QKT[:, g, tok(t)], CST[:, g], start=True, stop=True)
                    last.then_inc(s_int, 1)
                    pe.wait_ge(s_PT, t + 1)
                    if t >= 1:
                        pe.wait_ge(s_num, t)
                    for h in range(H):
                        last = pe.matmul(ps[6 + h // 4][:, (h % 4) * VA:(h % 4 + 1) * VA], PT[:, h], VAU[:, t, h], start=True, stop=True)
                    last.then_inc(s_intra, 1)
                    if t + 1 < TT:
                        scores(t + 1)
                    pe.wait_ge(s_kw, t + 1)
                    pe.wait_ge(s_tmp, t + 1)
                    for g in range(2):
                        last = pe.matmul(ps[4 + g][:, 0:4 * VA], kw[:, g * P:(g + 1) * P], VAU[:, t, 4 * g:4 * g + 4].rearrange("p h c -> p (h c)"), start=True, stop=True)
                    last.then_inc(s_upd, 1)

    r3w = Region(A_W, 64 * KB)
    KTT = r3w.take("KTT", [P, H, S])
    VS = r3w.take("VS", [P, TT, CH])
    PB = r3w.take("PB", [P, 2, S])
    PTS = r3w.take("PTS", [P, 2, TT, P])
    QTT = Region(A_RAW + 16 * KB, 32 * KB).take("QTT", [P, H, S])
    r3e = Region(E0, left - (E0 - A_E))
    qks = r3e.take("qks", [P, 2, H * AUG])
    mixf = r3e.take("mixf", [P, 2, CH])
    fsq = r3e.take("fsq", [P, CH])
    fw = r3e.take("fw", [P, CH])
    zeros = r3e.take("zeros", [P, CH])
    nmax = r3e.take("nmax", [P, 2])
    rowsum = r3e.take("rowsum", [P, 2, H])
    fsum = r3e.take("fsum", [P, 2, H])
    NU = TT * H
    USERS, MIXAT = [], 4
    for u_ in range(NU):
        USERS.append(("p", u_))
        if u_ >= H and u_ % H == MIXAT:
            USERS.append(("m", u_ // H - 1))
    USERS.append(("m", TT - 1))
    USER_OF = {x: i for i, x in enumerate(USERS)}
    ACT_OUT = []
    for kind_, i_ in USERS:
        ACT_OUT.append((ACT_OUT[-1] if ACT_OUT else 0) + (1 if kind_ == "p" and i_ // H >= 4 else 0))

    def stage3():
        def s3(n):
            return sem("s3_" + n)
        s_ld = [s3("ld0"), s3("ld1")]
        s_v, s_fw, s_qkt = s3("values"), s3("outw"), s3("qkt")
        s_ka, s_kd = s3("out_act"), s3("out_dve")
        s_S, s_msk, s_nmax, s_P, s_T, s_ptd, s_pta = s3("S"), s3("masked"), s3("nmax"), s3("P"), s3("T"), s3("pt_dve"), s3("pt_act")
        s_pv, s_o, s_fsq, s_fsum, s_mix, s_hi = s3("pv"), s3("o"), s3("fsq"), s3("fsum"), s3("mix"), s3("hi")
        s_ri, s_zero, s_filled = s3("ri"), s3("zero"), s3("filled")

        with nc.Block() as block:
            @block.sync
            def _(sp):
                for i in range(2 * TT):
                    if i >= 2:
                        sp.wait_ge(s_qkt, i - 1)
                    src = dK if i < TT else dQ
                    sp.dma_start(qks[:, i % 2], src[tok(i % TT), :]).then_inc(s_ld[i % 2], 16)
                sp.dma_start(VS[:], dV.rearrange("(t p) c -> p t c", p=P)).then_inc(s_v, 16)
                sp.wait_ge(s_zero, 1)
                for b in range(S * TOPK // P, SBMAX):
                    sp.dma_start(dY[b * P:(b + 1) * P, :].rearrange("p (a c) -> p a c", a=2), bc(zeros[:].unsqueeze(1), [P, 2, CH])).then_inc(s_filled, 16)
                sp.dma_start(fw[:], A["fox_out_norm_w"][0].partition_broadcast(P)).then_inc(s_fw, 16)
                sp.wait_ge(s_filled, 16 * (SBMAX - S * TOPK // P))

            @block.gpsimd
            def _(pool):
                link = chain(pool, "s3_pool")
                pool.memset(zeros[:], 0.0).then_inc(s_zero, 1)
                pool.wait_ge(s_fw, 16)
                for t in range(TT):
                    pool.wait_ge(s_fsum, t + 1)
                    link(inv_root(pool, link, fsum[:, t % 2], fsum[:, t % 2], HD))
                    y = mixf[:, t % 2]
                    yv = y.rearrange("p (h d) -> p h d", h=H)
                    link(pool.tensor_tensor(yv, yv, bc(fsum[:, t % 2].unsqueeze(2), [P, H, HD]), ALU.mult))
                    pool.tensor_tensor(y, y, fw[:], ALU.mult).then_inc(s_mix, 1)

            @block.scalar
            def _(act):
                for i in range(2 * TT):
                    act.wait_ge(s_qkt, i + 1)
                    to = KTT if i < TT else QTT
                    act.activation(to[0:AUG, 0:4, tok(i % TT)], ps[2 * (i % 2)][0:AUG].rearrange("p (h c) -> p h c", h=4), ACT.Copy).then_inc(s_ka, 1)

                def after(u):
                    t, h = u // H, u % H
                    if t >= 4:
                        act.wait_ge(s_T, USER_OF["p", u] + 1)
                        if u >= 2:
                            act.wait_ge(s_pv, u - 1)
                        act.activation(PTS[:, u % 2, 4:t + 1], ps[5][:, 0:(t - 3) * P].rearrange("p (t c) -> p t c", c=P), ACT.Copy).then_inc(s_pta, 1)
                    if u >= H and h == MIXAT:
                        mixed(t - 1)

                def mixed(t):
                    act.wait_ge(s_T, USER_OF["m", t] + 1)
                    for g in range(2):
                        last = act.activation(XH[:, 4 * g:4 * g + 4, tok(t)], ps[4 + g][:].rearrange("p (k c) -> p k c", k=4), ACT.Copy)
                    last.then_inc(s_hi, 1)

                for u in range(NU):
                    t, h = u // H, u % H
                    act.wait_ge(s_nmax, u + 1)
                    if u >= 2:
                        act.wait_ge(s_T, USER_OF["p", u - 2] + 1)
                    if t >= 2 and h == 0:
                        act.wait_ge(s_o, t - 1)
                    if t < 4:
                        act.activation(PB[:, u % 2, 0:(t + 1) * P], ps[2 * (u % 2)][:, 0:(t + 1) * P], ACT.Exp, bias=nmax[:, u % 2:u % 2 + 1],
                                       accum_out=rowsum[:, t % 2, h:h + 1]).then_inc(s_P, 1)
                    else:
                        act.activation(PB[:, u % 2, 0:(t + 1) * P], pair(u % 2, (t + 1) * P), ACT.Exp, bias=nmax[:, u % 2:u % 2 + 1],
                                       accum_out=rowsum[:, t % 2, h:h + 1]).then_inc(s_P, 1)
                    if u >= 1:
                        after(u - 1)
                    if h == 2 and t >= 1:
                        act.wait_ge(s_o, t)
                        if t >= 2:
                            act.wait_ge(s_fsum, t - 1)
                        act.activation(fsq[:], mixf[:, (t - 1) % 2], ACT.Square).then_inc(s_fsq, 1)
                after(NU - 1)
                act.wait_ge(s_o, TT)
                act.wait_ge(s_fsum, TT - 1)
                act.activation(fsq[:], mixf[:, (TT - 1) % 2], ACT.Square).then_inc(s_fsq, 1)
                mixed(TT - 1)

            @block.vector
            def _(dve):
                for i in range(2 * TT):
                    dve.wait_ge(s_qkt, i + 1)
                    to = KTT if i < TT else QTT
                    dve.tensor_copy(to[0:AUG, 4:8, tok(i % TT)], ps[2 * (i % 2) + 1][0:AUG].rearrange("p (h c) -> p h c", h=4)).then_inc(s_kd, 1)

                def after(u):
                    t, h = u // H, u % H
                    dve.wait_ge(s_T, USER_OF["p", u] + 1)
                    if u >= 2:
                        dve.wait_ge(s_pv, u - 1)
                    n = min(t + 1, 4)
                    dve.tensor_copy(PTS[:, u % 2, 0:n], ps[4][:, 0:n * P].rearrange("p (t c) -> p t c", c=P)).then_inc(s_ptd, 1)
                    if u >= H and h == MIXAT:
                        mixed(t - 1)

                def mixed(t):
                    dve.wait_ge(s_hi, t + 1)
                    for g in range(2):
                        last = dve.tensor_tensor(XL[:, 4 * g:4 * g + 4, tok(t)], ps[4 + g][:].rearrange("p (k c) -> p k c", k=4),
                                                 XH[:, 4 * g:4 * g + 4, tok(t)].bitcast(f32), ALU.subtract)
                    last.then_inc(s_ptd, 1)

                def outputs(t):
                    dve.wait_ge(s_pv, H * (t + 1))
                    dve.reciprocal(rowsum[:, t % 2], rowsum[:, t % 2]).then_inc(s_ri, 1)
                    dve.wait_ge(s_ri, t + 1)
                    if t >= 2:
                        dve.wait_ge(s_T, USER_OF["m", t - 2] + 1)
                    dve.tensor_tensor(mixf[:, t % 2].rearrange("p (h d) -> p h d", h=H), ps[6 + t % 2][:].rearrange("p (h d) -> p h d", h=H),
                                      bc(rowsum[:, t % 2].unsqueeze(2), [P, H, HD]), ALU.mult).then_inc(s_o, 1)

                def squares(t):
                    dve.wait_ge(s_fsq, t + 1)
                    dve.tensor_reduce(fsum[:, t % 2], fsq[:].rearrange("p (h c) -> p h c", h=H), X, ALU.add).then_inc(s_fsum, 1)

                for u in range(NU):
                    t, h = u // H, u % H
                    n = (t + 1) * P
                    dve.wait_ge(s_S, u + 1)
                    d = ps[2 * (u % 2) + (t // 4)][:, (t % 4) * P:(t % 4 + 1) * P]
                    dve.tensor_tensor(d, d, causal[:], ALU.add).then_inc(s_msk, 1)
                    dve.wait_ge(s_msk, u + 1)
                    if u >= 2:
                        dve.wait_ge(s_P, u - 1)
                    dve.tensor_reduce(nmax[:, u % 2:u % 2 + 1], pair(u % 2, n), X, ALU.max, negate=True).then_inc(s_nmax, 1)
                    if u >= 1:
                        after(u - 1)
                    if h == 1 and t >= 1:
                        outputs(t - 1)
                    if h == 3 and t >= 1:
                        squares(t - 1)
                after(NU - 1)
                outputs(TT - 1)
                squares(TT - 1)
                mixed(TT - 1)

            @block.tensor
            def _(pe):
                for i in range(2 * TT):
                    pe.wait_ge(s_ld[i % 2], 16 * (i // 2 + 1))
                    if i >= 2:
                        pe.wait_ge(s_ka, i - 1)
                        pe.wait_ge(s_kd, i - 1)
                    for h in range(H):
                        last = pe.transpose(ps[2 * (i % 2) + h // 4][0:AUG, (h % 4) * P:(h % 4 + 1) * P], qks[:, i % 2, h * AUG:(h + 1) * AUG], ident[:])
                    last.then_inc(s_qkt, 1)
                pe.wait_ge(s_ka, 2 * TT)
                pe.wait_ge(s_kd, 2 * TT)

                def scores(u):
                    t, h = u // H, u % H
                    if u >= 2:
                        pe.wait_ge(s_P, u - 1)
                    for g in range(t // 4 + 1):
                        n = min((t + 1) * P - g * CH, CH)
                        last = pe.matmul(ps[2 * (u % 2) + g][:, 0:n], QTT[0:AUG, h, tok(t)], KTT[0:AUG, h, g * CH:g * CH + n], start=True, stop=True)
                    last.then_inc(s_S, 1)

                def free_banks(i):
                    if i >= 1:
                        pe.wait_ge(s_ptd, i)
                        if ACT_OUT[i - 1]:
                            pe.wait_ge(s_pta, ACT_OUT[i - 1])

                def turn(u):
                    t = u // H
                    pe.wait_ge(s_P, u + 1)
                    free_banks(USER_OF["p", u])
                    for j in range(t + 1):
                        last = pe.transpose(ps[4 + j // 4][:, (j % 4) * P:(j % 4 + 1) * P], PB[:, u % 2, j * P:(j + 1) * P], ident[:])
                    last.then_inc(s_T, 1)
                    if u >= H and u % H == MIXAT:
                        mixed(t - 1)

                def mixed(t):
                    pe.wait_ge(s_mix, t + 1)
                    free_banks(USER_OF["m", t])
                    for k in range(KT):
                        src = mixf[:, t % 2, k * P:(k + 1) * P] if k < 4 else MY[:, t, (k - 4) * P:(k - 3) * P]
                        last = pe.transpose(ps[4 + k // 4][:, (k % 4) * P:(k % 4 + 1) * P], src, ident[:])
                    last.then_inc(s_T, 1)

                def values(u):
                    t, h = u // H, u % H
                    if t >= 2 and h == 0:
                        pe.wait_ge(s_o, t - 1)
                    pe.wait_ge(s_ptd, USER_OF["p", u] + 1)
                    if t >= 4:
                        pe.wait_ge(s_pta, ACT_OUT[USER_OF["p", u]])
                    for j in range(t + 1):
                        last = pe.matmul(ps[6 + t % 2][:, h * HD:(h + 1) * HD], PTS[:, u % 2, j], VS[:, j, h * HD:(h + 1) * HD], start=j == 0, stop=j == t)
                    last.then_inc(s_pv, 1)

                scores(0)
                scores(1)
                turn(0)
                pe.wait_ge(s_v, 16)
                for u in range(NU):
                    if u + 2 < NU:
                        scores(u + 2)
                    if u + 1 < NU:
                        turn(u + 1)
                    values(u)
                mixed(TT - 1)

    r4 = Region(A_RAW + 32 * KB, 16 * KB)
    wb4 = r4.take("wb4", [P, D])
    xr = r4.take("xr", [P, 2, D])
    h2T = r4.take("h2T", [P, KT, P])
    sqr4 = Region(A_RAW, 4 * KB).take("sqr4", [P, D])
    m8 = ext.take("m8", [P, TT, 8])
    pos = ext.take("pos", [P, TT * TOPK], u32)
    idxall = ext.take("idxall", [P, SBMAX + 1], u32)
    tab = ext.take("tab", [1, SBMAX + 2], i32)
    nblk = ext.take("nblk", [1, 1], i32)
    E1 = ext.at
    r4e = Region(E1, left - (E1 - A_E))
    x1 = r4e.take("x1", [P, 2, D])
    h2 = r4e.take("h2", [P, 2, D])
    rw = r4e.take("rw", [P, KT, NE])
    rb = r4e.take("rb", [P, NE])
    logits = r4e.take("logits", [P, TT, NE])

    def stage4():
        def s4(n):
            return sem("s4_" + n)
        s_raw, s_wb, s_rw, s_x, s_st = [s4("raw0"), s4("raw1")], s4("wb"), s4("rw"), [s4("x0"), s4("x1")], [s4("st0"), s4("st1")]
        s_sh = [s4("sh0"), s4("sh1")]
        s_hi, s_w, s_out, s_x1, s_ss, s_rs, s_h2, s_T, s_h2T, s_l, s_lg = (s4(n) for n in ("hi", "w", "out", "x1d", "ss", "rs", "h2", "T", "h2T", "l", "lg"))

        with nc.Block() as block:
            @block.sync
            def _(sp):
                for c in range(2):
                    sp.dma_start(RAW[:, c], w_out[:, :, c * CH:(c + 1) * CH]).then_inc(s_raw[c], 16)
                sp.dma_start(wb4[:], A["moe_norm_w"][0].partition_broadcast(P)).then_inc(s_wb, 16)
                sp.dma_start(rw[:], A["router_w"][0].rearrange("(k p) e -> p k e", p=P)).then_inc(s_rw, 16)
                sp.dma_start(rb[:], A["router_b"][0].partition_broadcast(P)).then_inc(s_rw, 16)
                for t in range(TT + 1):
                    if t < TT:
                        if t >= 2:
                            sp.wait_ge(s_x1, t - 1)
                        sp.dma_start(xr[:, t % 2], x2[tok(t), :]).then_inc(s_x[t % 2], 16)
                    if t >= 1:
                        sp.wait_ge(s_x1, t)
                        sp.dma_start(dX1[tok(t - 1), :], x1[:, (t - 1) % 2]).then_inc(s_st[(t - 1) % 2], 16)
                        sp.wait_ge(s_h2, t)
                        sp.dma_start(dH2[tok(t - 1), :], h2[:, (t - 1) % 2]).then_inc(s_sh[(t - 1) % 2], 16)
                for i in range(2):
                    sp.wait_ge(s_st[i], 16 * TT // 2)
                    sp.wait_ge(s_sh[i], 16 * TT // 2)

            @block.gpsimd
            def _(pool):
                link = chain(pool, "s4_pool")
                for t in range(TT):
                    pool.wait_ge(s_ss, t + 1)
                    r = rmsB[:, t:t + 1]
                    inv_root(pool, link, r, r, D).then_inc(s_rs, 1)

            @block.scalar
            def _(act):
                for c in range(2):
                    act.wait_ge(s_raw[c], 16)
                    act.activation(WH[:, c], RAW[:, c], ACT.Copy).then_inc(s_hi, 1)
                act.wait_ge(s_w, 1)
                for t in range(TT + 1):
                    if t < TT:
                        act.wait_ge(s_x1, t + 1)
                        if t >= 1:
                            act.wait_ge(s_ss, t)
                        act.activation(sqr4[:], x1[:, t % 2], ACT.Square, accum_out=rmsB[:, t:t + 1]).then_inc(s_ss, 1)
                    if t >= 1:
                        act.wait_ge(s_T, t)
                        if t >= 2:
                            act.wait_ge(s_l, t - 1)
                        act.activation(h2T[:].rearrange("p k c -> p (k c)"), pair(2, D), ACT.Copy).then_inc(s_h2T, 1)

            @block.vector
            def _(dve):
                for c in range(2):
                    dve.wait_ge(s_hi, c + 1)
                    dve.tensor_tensor(WL[:, c], RAW[:, c], WH[:, c].bitcast(f32), ALU.subtract).then_inc(s_w, 1)
                dve.wait_ge(s_wb, 16)
                dve.wait_ge(s_rw, 32)
                for t in range(TT):
                    dve.wait_ge(s_out, t + 1)
                    dve.wait_ge(s_x[t % 2], 16 * (t // 2 + 1))
                    if t >= 2:
                        dve.wait_ge(s_st[t % 2], 16 * (t // 2))
                        dve.wait_ge(s_ss, t - 1)
                    dve.tensor_tensor(x1[:, t % 2], xr[:, t % 2], pair(t % 2, D), ALU.add).then_inc(s_x1, 1)
                    dve.wait_ge(s_rs, t + 1)
                    if t >= 2:
                        dve.wait_ge(s_sh[t % 2], 16 * (t // 2))
                        dve.wait_ge(s_T, t - 1)
                    dve.scalar_tensor_tensor(out=h2[:, t % 2], in0=x1[:, t % 2], scalar=rmsB[:, t:t + 1], in1=wb4[:],
                                             op0=ALU.mult, op1=ALU.mult).then_inc(s_h2, 1)
                    if t >= 1:
                        dve.wait_ge(s_l, t)
                        dve.tensor_tensor(logits[:, t - 1], ps[6 + (t - 1) % 2][:, 0:NE], rb[:], ALU.add).then_inc(s_lg, 1)
                dve.wait_ge(s_l, TT)
                dve.tensor_tensor(logits[:, TT - 1], ps[6 + (TT - 1) % 2][:, 0:NE], rb[:], ALU.add).then_inc(s_lg, 1)

            @block.tensor
            def _(pe):
                pe.wait_ge(s_rw, 32)
                for t in range(TT + 1):
                    if t < TT:
                        if t >= 2:
                            pe.wait_ge(s_x1, t - 1)
                        for c in range(2):
                            pe.wait_ge(s_w, c + 1)
                            for k in range(KT):
                                last = mm3(pe, ps[2 * (t % 2) + c], XH[:, k, tok(t)], XL[:, k, tok(t)], WH[:, c, k], WL[:, c, k], k == 0, k == KT - 1)
                        last.then_inc(s_out, 1)
                    if t >= 1:
                        pe.wait_ge(s_h2, t)
                        if t >= 2:
                            pe.wait_ge(s_h2T, t - 1)
                        for k in range(KT):
                            last = pe.transpose(ps[4 + k // 4][:, (k % 4) * P:(k % 4 + 1) * P], h2[:, (t - 1) % 2, k * P:(k + 1) * P], ident[:])
                        last.then_inc(s_T, 1)
                        pe.wait_ge(s_h2T, t)
                        if t >= 3:
                            pe.wait_ge(s_lg, t - 2)
                        for k in range(KT):
                            last = pe.matmul(ps[6 + (t - 1) % 2][:, 0:NE], h2T[:, k], rw[:, k], start=k == 0, stop=k == KT - 1)
                        last.then_inc(s_l, 1)

    r5 = Region(A_W, 64 * KB)
    ix8 = r5.take("ix8", [P, TT, 8], u32)
    ixf = r5.take("ixf", [P, TT * TOPK])
    iotaE = r5.take("iotaE", [P, NE])
    sel = r5.take("sel", [P, TT * TOPK, NE])
    selS = r5.take("selS", [P, TT, NE])
    prod = r5.take("prod", [P, TT * TOPK, NE])
    posf = r5.take("posf", [P, TT * TOPK])
    rank = r5.take("rank", [P, TT, NE])
    cnt = r5.take("cnt", [P, NE])
    nb = r5.take("nb", [P, NE])
    be = r5.take("be", [P, NE])
    bs = r5.take("bs", [P, NE])
    le = r5.take("le", [P, NE])
    srow = r5.take("srow", [P, 1])
    eidf = r5.take("eidf", [P, 1])
    eidi = r5.take("eidi", [P, 1], i32)
    nbi = r5.take("nbi", [P, 1], i32)
    onesE = r5.take("onesE", [P, NE])
    gsum = r5.take("gsum", [P, TT])
    g4 = ext.take("g4", [P, TT, TOPK])
    tokid = r5.take("tokid", [P, TT])
    zrow = r5.take("zrow", [P, P])
    tokr = r5.take("tokr", [P, P])

    def stage5():
        def s5(n):
            return sem("s5_" + n)
        s_it, s_sel, s_rank, s_pos, s_zd, s_sc, s_tk, s_tT, s_e = (s5(n) for n in ("iota", "sel", "rank", "pos", "zeroed", "scat", "tok", "tokT", "exp"))
        s_m, s_tab, s_tb, s_tb2, s_ix, s_z = s5("m"), s5("tabs"), s5("tabd"), s5("tabl"), s5("idx"), s5("z")

        with nc.Block() as block:
            @block.sync
            def _(sp):
                sp.wait_ge(s_z, 1)
                sp.dma_start(dTok.rearrange("(s p) a -> s (p a)", p=P), zrow[0:SBMAX]).then_inc(s_zd, 16)
                sp.wait_ge(s_tab, 1)
                sp.dma_start(dTab, eidi[0:SBMAX]).then_inc(s_tb, 16)
                sp.dma_start(dN, nbi[0:1]).then_inc(s_tb, 16)
                sp.wait_ge(s_tb, 32)
                sp.dma_start(tab[0:1, 0:SBMAX], dTab.rearrange("s a -> a s")).then_inc(s_tb2, 16)
                sp.dma_start(nblk[:], dN).then_inc(s_tb2, 16)
                sp.wait_ge(s_sc, 16 * TT * TOPK)
                sp.dma_start(tokr[0:SBMAX], dTok.rearrange("(s p) a -> s (p a)", p=P)).then_inc(s_tk, 16)
                sp.wait_ge(s_tb2, 32)

            @block.gpsimd
            def _(pool):
                pool.memset(zrow[:], 0.0).then_inc(s_z, 1)
                pool.memset(tab[:], 0)
                pool.iota(iotaE[:], pattern=[[1, NE]], base=0, channel_multiplier=0, allow_small_or_imprecise_dtypes=True)
                pool.iota(srow[:], pattern=[[1, 1]], base=0, channel_multiplier=1, allow_small_or_imprecise_dtypes=True)
                pool.iota(tokid[:], pattern=[[P, TT]], base=0, channel_multiplier=1, allow_small_or_imprecise_dtypes=True).then_inc(s_it, 1)
                pool.wait_ge(s_it, 1)
                pool.wait_ge(s_pos, 1)
                pool.wait_ge(s_zd, 16)
                for i in range(TT * TOPK):
                    pool.indirect_dma_start(dTok, bass.IndirectOffsetOnAxis(ap=pos[:, i:i + 1], axis=0),
                                            tokid[:, i // TOPK:i // TOPK + 1], None).then_inc(s_sc, 16)
                pool.wait_ge(s_sc, 16 * TT * TOPK)

            @block.scalar
            def _(act):
                act.wait_ge(s_m, 1)
                act.activation(g4[:], g4[:], ACT.Exp).then_inc(s_e, 1)

            @block.vector
            def _(dve):
                link = chain(dve, "s5_dve")
                for t in range(TT):
                    link(dve.max(m8[:, t], logits[:, t]))
                    link(dve.max_index(ix8[:, t], m8[:, t], logits[:, t]))
                dve.tensor_tensor(g4[:], m8[:, :, 0:TOPK], bc(m8[:, :, 0:1], [P, TT, TOPK]), ALU.subtract).then_inc(s_m, 1)
                link(dve.tensor_copy(ixf[:].rearrange("p (t k) -> p t k", k=TOPK), ix8[:, :, 0:TOPK]))
                dve.wait_ge(s_it, 1)
                link(dve.tensor_tensor(sel[:], bc(iotaE[:].unsqueeze(1), [P, TT * TOPK, NE]), bc(ixf[:].unsqueeze(2), [P, TT * TOPK, NE]), ALU.is_equal))
                dve.tensor_reduce(selS[:], sel[:].rearrange("p (t k) e -> p t e k", k=TOPK), X, ALU.add).then_inc(s_sel, 1)
                dve.memset(onesE[:], 1.0)
                dve.wait_ge(s_rank, 1)
                link(dve.tensor_copy(cnt[:], ps[1][:, 0:NE]))
                link(dve.tensor_scalar(nb[:], cnt[:], 0.0, None, ALU.is_gt))
                for j in range(1, S // P):
                    link(dve.scalar_tensor_tensor(out=nb[:], in0=cnt[:], scalar=float(j * P), in1=nb[:], op0=ALU.is_gt, op1=ALU.add))
                link(dve.tensor_tensor_scan(be[:], onesE[:], nb[:], 0.0, ALU.mult, ALU.add))
                link(dve.tensor_tensor(bs[:], be[:], nb[:], ALU.subtract))
                link(dve.scalar_tensor_tensor(out=rank[:], in0=bc(bs[:].unsqueeze(1), [P, TT, NE]), scalar=float(P), in1=ps[0][:, 0:TT * NE].rearrange("p (t e) -> p t e", e=NE), op0=ALU.mult, op1=ALU.add))
                for k in range(TOPK):
                    last = dve.tensor_tensor(prod[:].rearrange("p (t k) e -> p t k e", k=TOPK)[:, :, k], sel[:].rearrange("p (t k) e -> p t k e", k=TOPK)[:, :, k], rank[:], ALU.mult)
                link(last)
                link(dve.tensor_reduce(posf[:], prod[:], X, ALU.add))
                dve.tensor_copy(pos[:], posf[:]).then_inc(s_pos, 1)
                link(dve.tensor_scalar(le[:], be[:], srow[:, 0:1], None, ALU.is_le))
                link(dve.tensor_reduce(eidf[:], le[:], X, ALU.add))
                link(dve.tensor_scalar(eidf[:], eidf[:], float(NE - 1), None, ALU.min))
                dve.tensor_copy(eidi[:], eidf[:])
                dve.tensor_copy(nbi[:], be[:, NE - 1:NE]).then_inc(s_tab, 1)
                dve.wait_ge(s_e, 1)
                link(dve.tensor_reduce(gsum[:], g4[:], X, ALU.add))
                link(dve.reciprocal(gsum[:], gsum[:]))
                dve.tensor_tensor(g4[:], g4[:], bc(gsum[:].unsqueeze(2), [P, TT, TOPK]), ALU.mult)
                dve.memset(idxall[:, SBMAX:SBMAX + 1], 0)
                dve.wait_ge(s_tT, 1)
                dve.tensor_copy(idxall[:, 0:SBMAX], ps[2][:, 0:SBMAX]).then_inc(s_ix, 1)

            @block.tensor
            def _(pe):
                pe.wait_ge(s_sel, 1)
                for t in range(TT):
                    o = ps[0][:, t * NE:(t + 1) * NE]
                    for j in range(t):
                        pe.matmul(o, ones[:], selS[:, j], start=j == 0, stop=False)
                    pe.matmul(o, before[:], selS[:, t], start=t == 0, stop=True)
                for j in range(TT):
                    last = pe.matmul(ps[1][:, 0:NE], ones[:], selS[:, j], start=j == 0, stop=j == TT - 1)
                last.then_inc(s_rank, 1)
                pe.wait_ge(s_tk, 16)
                pe.transpose(ps[2][:, 0:SBMAX], tokr[0:SBMAX], ident[0:SBMAX, 0:SBMAX]).then_inc(s_tT, 1)

    w_gu = A["expert_w_gate_up"][0].rearrange("e (k p) n -> e p k n", p=P)
    w_dn = A["expert_w_down"][0].rearrange("e (k p) n -> e p k n", p=P)
    b_gu, b_dn = A["expert_b_gate_up"][0], A["expert_b_down"][0]
    r6 = Region(A_X, 128 * KB)
    VH = r6.take("VH", [P, 3, KT, CH], f32r)
    VL = r6.take("VL", [P, 3, KT, CH], f32r)
    TH = r6.take("TH", [P, KT, P], f32r)
    TL = r6.take("TL", [P, KT, P], f32r)
    AH = r6.take("AH", [P, KT, P], f32r)
    AL = r6.take("AL", [P, KT, P], f32r)
    gu = r6.take("gu", [P, CH])
    sg = r6.take("sg", [P, HC])
    qa = r6.take("qa", [P, 2, HC])
    ys = r6.take("ys", [P, 2, CH])
    r6e = Region(ext.at, nc.sbuf_usable_end - ext.at)
    brow = r6e.take("brow", [1, 3 * D])
    bb = r6e.take("bb", [P, 2, CH])
    xg = r6e.take("xg", [P, D])
    icur = r6e.take("icur", [P, 1], u32)
    HK = KT // 2

    def stage6():
        def s6(n):
            return sem("s6_" + n)
        s_raw = [s6(f"raw{i}") for i in range(3)]
        s_hi, s_w = s6("hi"), s6("w")
        s_mm = s6("mm")
        s_b, s_bb = s6("bias"), s6("bb")
        s_waited = s6("waited")
        s_ic, s_xg, s_xT, s_xhi, s_x = s6("ic"), s6("xg"), s6("xT"), s6("xhi"), s6("x")
        s_gu, s_clip, s_sg, s_q = s6("gu"), s6("clip"), s6("sg"), s6("q")
        s_a, s_aT, s_ahi, s_act = s6("a"), s6("aT"), s6("ahi"), s6("act")
        s_y, s_ys, s_y0 = s6("y"), [s6("ys0"), s6("ys1")], s6("y0")

        with nc.Block() as block:
            @block.sync
            def _(sp):
                n_blocks = sp.value_load(nblk[0:1, 0:1], min_val=1, max_val=SBMAX)

                def load(c, e):
                    for g in range(2):
                        if c < GU:
                            dst = RAW[:, c % 3, :, g * HC:(g + 1) * HC]
                            src = w_gu[bass.ds(e, 1), :, :, g * D + c * HC:g * D + (c + 1) * HC]
                        else:
                            dst = RAW[:, c % 3, g * HK:(g + 1) * HK]
                            src = w_dn[bass.ds(e, 1), :, g * HK:(g + 1) * HK, (c - GU) * CH:(c - GU + 1) * CH]
                        sp.dma_start(dst, src.rearrange("a p k n -> p (a k) n")).then_inc(s_raw[c % 3], 16)

                def biases(e):
                    sp.dma_start(brow[0:1, 0:2 * D], b_gu[bass.ds(e, 1), :]).then_inc(s_b, 16)
                    sp.dma_start(brow[0:1, 2 * D:3 * D], b_dn[bass.ds(e, 1), :]).then_inc(s_b, 16)

                e0 = sp.value_load(tab[0:1, 0:1], min_val=0, max_val=NE - 1)
                for c in range(3):
                    load(c, e0)
                    if c == 0:
                        biases(e0)
                with sp.Fori(0, SBMAX) as s:
                    with sp.If(s < n_blocks):
                        e = sp.value_load(tab[0:1, bass.ds(s, 1)], min_val=0, max_val=NE - 1)
                        en = sp.value_load(tab[0:1, bass.ds(s + 1, 1)], min_val=0, max_val=NE - 1)
                        for c in range(NCH):
                            sp.wait_ge(s_w, s * (2 * NCH) + (2 * c + 2))
                            load((c + 3) % NCH, e if c + 3 < NCH else en)
                        sp.wait_ge(s_bb, s * NCH + NCH)
                        biases(en)
                    with sp.Else():
                        sp.nop()
                for i in range(3):
                    sp.wait_ge(s_raw[i], n_blocks * 64 + 32)
                sp.wait_ge(s_b, n_blocks * 32 + 32)
                for j in range(2):
                    sp.wait_ge(s_ys[j], n_blocks * 16 + 16)
                sp.sem_inc(s_waited, 1)

            @block.gpsimd
            def _(pool):
                def wait(s_, value):
                    pool.wait_ge(s_, value)
                    pool.sem_inc(s_waited, 1)

                n_blocks = pool.value_load(nblk[0:1, 0:1], min_val=1, max_val=SBMAX)

                def gather():
                    pool.indirect_dma_start(xg[:], None, dH2, bass.IndirectOffsetOnAxis(ap=icur[:, 0:1], axis=0)).then_inc(s_xg, 16)

                pool.tensor_copy(icur[:], idxall[:, 0:1]).then_inc(s_ic, 1)
                pool.wait_ge(s_ic, 1)
                gather()
                with pool.Fori(0, SBMAX) as s:
                    with pool.If(s < n_blocks):
                        wait(s_xT, s + 1)
                        pool.tensor_copy(icur[:], idxall[:, bass.ds(s + 1, 1)]).then_inc(s_ic, 1)
                        wait(s_ic, s + 2)
                        gather()
                        wait(s_b, s * 32 + 32)
                        for c in range(NCH):
                            if c < 2:
                                wait(s_y, s * 2 + (c + 1))
                            else:
                                wait(s_gu, s * GU + (c + 1))
                            if c < GU:
                                for g in range(2):
                                    last = pool.partition_broadcast(bb[:, c % 2, g * HC:(g + 1) * HC], brow[0:1, g * D + c * HC:g * D + (c + 1) * HC], P)
                            else:
                                last = pool.partition_broadcast(bb[:, c % 2], brow[0:1, 2 * D + (c - GU) * CH:2 * D + (c - GU + 1) * CH], P)
                            last.then_inc(s_bb, 1)
                            if c < GU:
                                wait(s_gu, s * GU + (c + 3))
                                pool.tensor_scalar(gu[:, 0:HC], gu[:, 0:HC], LIMIT, -3.0e38, ALU.min, ALU.max)
                                pool.tensor_scalar(gu[:, HC:CH], gu[:, HC:CH], LIMIT, -LIMIT, ALU.min, ALU.max).then_inc(s_clip, 1)
                    with pool.Else():
                        pool.nop()
                wait(s_xg, n_blocks * 16 + 16)

            @block.scalar
            def _(act):
                n_blocks = act.value_load(nblk[0:1, 0:1], min_val=1, max_val=SBMAX)

                def split_hi(i, arrived):
                    act.wait_ge(s_raw[i], arrived)
                    for hf in range(2):
                        ks = slice(hf * HK, (hf + 1) * HK)
                        act.activation(VH[:, i, ks], RAW[:, i, ks], ACT.Copy).then_inc(s_hi, 1)

                def tokens_hi(count):
                    act.wait_ge(s_xT, count)
                    act.activation(TH[:].rearrange("p k c -> p (k c)"), pair(3, D), ACT.Copy).then_inc(s_xhi, 1)

                def act_hi(s, c):
                    act.wait_ge(s_aT, s * GU + (c + 1))
                    act.activation(AH[:, 2 * c:2 * c + 2].rearrange("p k c -> p (k c)"), ps[4 + c % 2][:, 0:HC], ACT.Copy).then_inc(s_ahi, 1)

                act.wait_ge(s_y0, 1)
                for j in range(2):
                    act.dma_start(dY[0:P, j * CH:(j + 1) * CH], ys[:, j]).then_inc(s_ys[j], 16)
                split_hi(0, 32)
                split_hi(1, 32)
                tokens_hi(1)
                with act.Fori(0, SBMAX) as s:
                    with act.If(s < n_blocks):
                        for c in range(NCH):
                            n2 = c + 2
                            act.wait_ge(s_mm, s * NCH + (c + 1))
                            split_hi(n2 % 3, s * 64 + 32 * (n2 // 3 + 1))
                            if 1 <= c <= GU:
                                act_hi(s, c - 1)
                            if c < GU:
                                act.wait_ge(s_clip, s * GU + (c + 1))
                                act.wait_ge(s_a, s * GU + (c + 1))
                                act.activation(sg[:], gu[:, 0:HC], ACT.Sigmoid, scale=ALPHA).then_inc(s_sg, 1)
                                if c == GU - 1:
                                    tokens_hi(s + 2)
                            else:
                                j = c - GU
                                act.wait_ge(s_y, s * 2 + (j + 3))
                                act.dma_start(dY[bass.ds(s * P, P), j * CH:(j + 1) * CH], ys[:, j]).then_inc(s_ys[j], 16)
                    with act.Else():
                        act.nop()

            @block.vector
            def _(dve):
                n_blocks = dve.value_load(nblk[0:1, 0:1], min_val=1, max_val=SBMAX)

                def split_lo(i, rounded):
                    for hf in range(2):
                        dve.wait_ge(s_hi, rounded + hf)
                        ks = slice(hf * HK, (hf + 1) * HK)
                        dve.tensor_tensor(VL[:, i, ks], RAW[:, i, ks], VH[:, i, ks].bitcast(f32), ALU.subtract).then_inc(s_w, 1)

                def tokens_lo(count):
                    dve.wait_ge(s_xhi, count)
                    dve.tensor_tensor(TL[:].rearrange("p k c -> p (k c)"), pair(3, D), TH[:].rearrange("p k c -> p (k c)").bitcast(f32), ALU.subtract).then_inc(s_x, 1)

                def act_lo(s, c):
                    dve.wait_ge(s_ahi, s * GU + (c + 1))
                    dve.tensor_tensor(AL[:, 2 * c:2 * c + 2].rearrange("p k c -> p (k c)"), ps[4 + c % 2][:, 0:HC],
                                      AH[:, 2 * c:2 * c + 2].rearrange("p k c -> p (k c)").bitcast(f32), ALU.subtract).then_inc(s_act, 1)

                dve.memset(ys[:], 0.0).then_inc(s_y0, 1)
                dve.sem_inc(s_a, 1)
                dve.sem_inc(s_gu, 2)
                dve.sem_inc(s_act, 2)
                dve.sem_inc(s_y, 2)
                split_lo(0, 1)
                split_lo(1, 3)
                tokens_lo(1)
                with dve.Fori(0, SBMAX) as s:
                    with dve.If(s < n_blocks):
                        for c in range(NCH):
                            split_lo((c + 2) % 3, s * (2 * NCH) + (2 * (c + 2) + 1))
                            if c == GU:
                                act_lo(s, c - 1)
                            dve.wait_ge(s_mm, s * NCH + (c + 2))
                            dve.wait_ge(s_bb, s * NCH + (c + 1))
                            if c < GU:
                                dve.wait_ge(s_a, s * GU + (c + 1))
                                dve.tensor_tensor(gu[:], ps[c % 2], bb[:, c % 2], ALU.add).then_inc(s_gu, 1)
                                if c >= 1:
                                    act_lo(s, c - 1)
                                dve.wait_ge(s_clip, s * GU + (c + 1))
                                dve.wait_ge(s_sg, s * GU + (c + 1))
                                dve.tensor_tensor(sg[:], gu[:, 0:HC], sg[:], ALU.mult).then_inc(s_q, 1)
                                dve.wait_ge(s_q, s * GU + (c + 1))
                                dve.scalar_tensor_tensor(out=qa[:, c % 2], in0=gu[:, HC:CH], scalar=1.0, in1=sg[:], op0=ALU.add, op1=ALU.mult).then_inc(s_a, 1)
                                if c == GU - 1:
                                    tokens_lo(s + 2)
                            else:
                                j = c - GU
                                dve.wait_ge(s_ys[j], s * 16 + 16)
                                dve.tensor_tensor(ys[:, j], ps[2 + j], bb[:, c % 2], ALU.add).then_inc(s_y, 1)
                    with dve.Else():
                        dve.nop()

            @block.tensor
            def _(pe):
                n_blocks = pe.value_load(nblk[0:1, 0:1], min_val=1, max_val=SBMAX)

                def tokens(count):
                    pe.wait_ge(s_xg, count * 16)
                    for k in range(KT):
                        last = pe.transpose(ps[6 + k // 4][:, (k % 4) * P:(k % 4 + 1) * P], xg[:, k * P:(k + 1) * P], ident[:])
                    last.then_inc(s_xT, 1)

                def product(s, o, c, lh, ll, ks):
                    for k in ks:
                        if k % HK == 0:
                            pe.wait_ge(s_w, s * (2 * NCH) + (2 * c + 1 + k // HK))
                        last = mm3(pe, o, lh[:, k], ll[:, k], VH[:, c % 3, k], VL[:, c % 3, k], k == 0, k == KT - 1)
                    return last

                def turned(s, c):
                    pe.wait_ge(s_a, s * GU + (c + 2))
                    pe.wait_ge(s_act, s * GU + (c + 1))
                    for i in range(2):
                        last = pe.transpose(ps[4 + c % 2][:, i * P:(i + 1) * P], qa[:, c % 2, i * P:(i + 1) * P], ident[:])
                    last.then_inc(s_aT, 1)

                pe.sem_inc(s_mm, 1)
                tokens(1)
                with pe.Fori(0, SBMAX) as s:
                    with pe.If(s < n_blocks):
                        pe.wait_ge(s_x, s + 1)
                        for c in range(GU):
                            pe.wait_ge(s_gu, s * GU + (c + 1))
                            product(s, ps[c % 2], c, TH, TL, range(KT)).then_inc(s_mm, 1)
                            if c >= 1:
                                turned(s, c - 1)
                        tokens(s + 2)
                        pe.wait_ge(s_y, s * 2 + 1)
                        pe.wait_ge(s_act, s * GU + (GU + 1))
                        product(s, ps[2], GU, AH, AL, range(KT - 2))
                        turned(s, GU - 1)
                        pe.wait_ge(s_act, s * GU + (GU + 2))
                        product(s, ps[2], GU, AH, AL, range(KT - 2, KT)).then_inc(s_mm, 1)
                        pe.wait_ge(s_y, s * 2 + 2)
                        product(s, ps[3], GU + 1, AH, AL, range(KT)).then_inc(s_mm, 1)
                    with pe.Else():
                        pe.nop()

    r7 = Region(A_X, 128 * KB)
    yk = r7.take("yk", [P, 2, TOPK, D])
    acc = r7.take("acc", [P, 2, D])

    def stage7():
        def s7(n):
            return sem("s7_" + n)
        s_x, s_k, s_a, s_o = [s7("x0"), s7("x1")], [s7("y0"), s7("y1")], s7("acc"), [s7("out0"), s7("out1")]

        with nc.Block() as block:
            @block.sync
            def _(sp):
                for t in range(TT + 1):
                    if t < TT:
                        if t >= 2:
                            sp.wait_ge(s_o[t % 2], 16 * (t // 2))
                        sp.dma_start(acc[:, t % 2], dX1[tok(t), :]).then_inc(s_x[t % 2], 16)
                    if t >= 1:
                        sp.wait_ge(s_a, TOPK * t)
                        sp.dma_start(out2[tok(t - 1), :], acc[:, (t - 1) % 2]).then_inc(s_o[(t - 1) % 2], 16)
                for i in range(2):
                    sp.wait_ge(s_o[i], 16 * TT // 2)

            @block.gpsimd
            def _(pool):
                for t in range(TT):
                    if t >= 2:
                        pool.wait_ge(s_a, TOPK * (t - 1))
                    for k in range(TOPK):
                        pool.indirect_dma_start(yk[:, t % 2, k], None, dY, bass.IndirectOffsetOnAxis(ap=pos[:, t * TOPK + k:t * TOPK + k + 1], axis=0)).then_inc(s_k[t % 2], 16)

            @block.vector
            def _(dve):
                for t in range(TT):
                    dve.wait_ge(s_x[t % 2], 16 * (t // 2 + 1))
                    dve.wait_ge(s_k[t % 2], 16 * TOPK * (t // 2 + 1))
                    for k in range(TOPK):
                        dve.scalar_tensor_tensor(out=acc[:, t % 2], in0=yk[:, t % 2, k], scalar=g4[:, t, k:k + 1], in1=acc[:, t % 2],
                                                 op0=ALU.mult, op1=ALU.add).then_inc(s_a, 1)
                        dve.wait_ge(s_a, TOPK * t + k + 1)

    for stage_ in (stage1, stage2, stage3, stage4, stage5, stage6, stage7):
        run(stage_)


_INS = ["x", "attn_norm_w", "w_in", "fox_f_bias", "fox_q_norm_w", "fox_k_norm_w", "fox_out_norm_w", "mlstm_conv_w",
        "mlstm_i_bias", "mlstm_f_bias", "mlstm_out_norm_w", "w_out", "moe_norm_w", "router_w", "router_b",
        "expert_w_gate_up", "expert_b_gate_up", "expert_w_down", "expert_b_down"]


def kernel(**inputs):
    import numpy as _np
    import concourse.bacc as _bacc
    from concourse import mybir as _mybir
    from concourse.bass_utils import run_bass_kernel_spmd as _run

    nc = _bacc.Bacc("TRN2", target_bir_lowering=False, num_devices=1)
    arrays, args = {}, {}
    for name in _INS:
        a = _np.ascontiguousarray(inputs[name])
        arrays[f"in_{name}"] = a
        args[name] = nc.dram_tensor(f"in_{name}", a.shape, _mybir.dt.from_np(a.dtype), kind="ExternalInput").ap()
    out = nc.dram_tensor("out_0", (1, S, D), _mybir.dt.float32, kind="ExternalOutput").ap()
    layer_kernel(nc, args, out)
    r = _run(nc, [arrays], core_ids=[0])
    return r.results[0]["out_0"]
```

```python
from contextlib import ExitStack
import concourse.bass as bass
from concourse import mybir

P = 128
D = 1024
S = 1024
TT = S // P
KT = D // P
H = 8
HD = 64
QK = 32
AUG = HD + 2
VA = HD + 1
NE = 32
TOPK = 4
CH = 512
W_IN = 3096
EPS = 1e-5
ALPHA = 1.702
LIMIT = 7.0
NEG = -1e30
SBMAX = S * TOPK // P + NE
SLOTS = SBMAX * P
SSB = S * TOPK // (2 * P) + NE
NCH = 6
GU = 4
HC = CH // 2

C_FQ, C_FK, C_FV, C_FF, C_MQ, C_MV, C_MI, C_MF, C_MO = 0, 512, 1024, 1536, 1544, 2056, 2568, 2576, 2584


def layer_kernel(nc, A, out):
    f32, f32r, i32, u32 = mybir.dt.float32, mybir.dt.float32r, mybir.dt.int32, mybir.dt.uint32
    ALU, ACT, AX = mybir.AluOpType, mybir.ActivationFunctionType, mybir.AxisListType
    X = AX.X

    base = (nc.sbuf_base + 63) // 64 * 64
    KB = 1024
    A_X = base
    A_W = A_X + 64 * KB
    A_RAW = A_W + 64 * KB
    A_E = A_RAW + 48 * KB

    class Region:
        def __init__(self, at, size):
            self.at, self.end = at, at + size

        def take(self, name, shape, dt=f32):
            n = 4
            for d in shape[1:]:
                n *= d
            t = nc.alloc_sbuf_tensor_at(name, shape, dt, offset=self.at)
            self.at += (n + 63) // 64 * 64
            assert self.at <= self.end, name
            return t

    rx = Region(A_X, 64 * KB)
    XH = rx.take("XH", [P, KT, S], f32r)
    XL = rx.take("XL", [P, KT, S], f32r)
    rw = Region(A_W, 64 * KB)
    WH = rw.take("WH", [P, 2, KT, CH], f32r)
    WL = rw.take("WL", [P, 2, KT, CH], f32r)
    RAW = Region(A_RAW, 48 * KB).take("RAW", [P, 3, KT, CH])

    left = nc.sbuf_usable_end - A_E
    ext = Region(A_E, left)
    ident = ext.take("ident", [P, P])
    ones = ext.take("ones", [P, P])
    before = ext.take("before", [P, P])
    causal = ext.take("causal", [P, P])
    causalT = ext.take("causalT", [P, P])
    half = ext.take("half", [P, H])
    onec = ext.take("onec", [P, 1])
    rmsA = ext.take("rmsA", [P, TT])
    rmsB = ext.take("rmsB", [P, TT])
    A_TR = ext.at
    TR = ext.take("TR", [P, TT, P])
    E0 = ext.at
    r1 = Region(E0, left - (E0 - A_E))
    xin = r1.take("xin", [P, 2, D])
    xn = r1.take("xn", [P, 2, D])
    r1b = Region(E0, 16 * KB + 256)
    zg = r1b.take("zg", [P, S])
    lf = r1b.take("lf", [P, S])
    cum = r1b.take("cum", [P, S])
    gt = r1b.take("gt", [P, S])
    SR = 3
    stage = r1.take("stage", [P, SR, H, AUG])
    gb = r1.take("gb", [P, 1])
    ssq = r1.take("ssq", [P, 2, H])
    rsq = r1.take("rsq", [P, 2, H])
    qkw = r1.take("qkw", [P, 2, HD])
    r1c = Region(A_RAW + 32 * KB, 16 * KB)
    wb1 = r1c.take("wb1", [P, D])
    GH = r1c.take("GH", [P, KT, P], f32r)
    GL = r1c.take("GL", [P, KT, P], f32r)
    R = r1c.take("R", [P, S])
    graw = Region(A_W + 48 * KB, 4 * KB).take("graw", [P, KT, P])
    sqr = Region(A_W + 52 * KB, 4 * KB).take("sqr", [P, D])
    sq = r1.take("sq", [P, CH])

    bank_pairs = [nc.alloc_psum_tensor(f"banks{2 * i}_{2 * i + 1}", [P, 2 * CH], f32) for i in range(4)]
    ps = [bank_pairs[i // 2][:, (i % 2) * CH:(i % 2 + 1) * CH] for i in range(8)]

    def pair(i, n):
        return bank_pairs[i][:, 0:n]

    def dram(name, shape, dt=f32):
        return nc.dram_tensor(name, shape, dt, kind="Internal").ap()
    dQ, dK = dram("dQ", [S, H * AUG]), dram("dK", [S, H * AUG])
    dV, dMV, dMO = dram("dV", [S, CH]), dram("dMV", [S, CH]), dram("dMO", [S, CH])
    dQK = dram("dQK", [4 * P, S])
    dX1, dH2 = dram("dX1", [S, D]), dram("dH2", [S, D])
    dTok = dram("dTok", [SLOTS, 1])
    dY = dram("dY", [SLOTS, D])
    dTab = dram("dTab", [SSB + 1, 3], i32)
    dN = dram("dN", [1, 1], i32)

    x2 = A["x"].rearrange("b s d -> (b s) d")
    w_in = A["w_in"][0].rearrange("(k p) n -> p k n", p=P)
    w_out = A["w_out"][0].rearrange("(k p) n -> p k n", p=P)
    out2 = out.rearrange("b s d -> (b s) d")

    held = []

    def sem(name):
        held.append(nc.alloc_semaphore(name))
        return held[-1]

    def run(stage_):
        held.clear()
        stage_()
        nc.clear_and_free_semaphores(list(held))
        nc.all_engine_barrier(sem_only=True)

    def tok(t):
        return slice(t * P, (t + 1) * P)

    def bc(ap, shape):
        return ap.broadcast_to(shape)

    def mm3(pe, o, lh, ll, rh, rl, start, stop):
        pe.matmul(o, lh, rh, start=start, stop=False)
        pe.matmul(o, lh, rl, start=False, stop=False)
        return pe.matmul(o, ll, rh, start=False, stop=stop)

    def chain(eng, name):
        s, n = sem(name), [0]

        def link(ins):
            n[0] += 1
            ins.then_inc(s, 1)
            eng.wait_ge(s, n[0])
        return link

    def inv_root(pool, link, o, sums, n):
        link(pool.tensor_scalar(o, sums, 1.0 / n, EPS, ALU.mult, ALU.add))
        return pool.tensor_tensor(o, o, half[:, 0:o.shape[1]], ALU.pow)

    KINDS = ("q", "k", "v", "mv", "qk", "mo")
    COLS = (C_FQ, C_FK, C_FV, C_MV, C_MQ, C_MO)
    READER = {"q": "dve", "k": "dve", "v": "act", "mv": "act", "qk": "act", "mo": "act"}
    OUTS = [("g", 0), ("g", 1)] + [(k, j) for k in KINDS for j in range(TT)]
    RING = 6
    reads = {"dve": 0, "act": 0}
    FREED = []
    for kind, _ in OUTS:
        e = READER.get(kind, "dve")
        reads[e] += 1
        FREED.append((e, reads[e]))
    STAGED = [(k, j) for k in KINDS for j in range(TT)]
    UNITS = range(len(STAGED))

    def stage1():
        s_x = [sem("s1_x0"), sem("s1_x1")]
        s_c, s_zero, s_gw, s_qkw = sem("s1_const"), sem("s1_zero"), sem("s1_gatew"), sem("s1_qkw")
        s_wb = sem("s1_wb")
        s_ss, s_rstd, s_xn, s_tp, s_hi, s_hT = (sem("s1_" + n) for n in ("ss", "rstd", "xn", "tp", "hi", "hT"))
        s_ghi, s_g = sem("s1_ghi"), sem("s1_g")
        s_raw = [sem("s1_raw0"), sem("s1_raw1")]
        s_whi, s_w, s_wused = sem("s1_whi"), sem("s1_w"), sem("s1_wused")
        s_out = sem("s1_out")
        s_free = {"dve": sem("s1_freed_dve"), "act": sem("s1_freed_act")}
        s_sq, s_ssq, s_rsq = sem("s1_sq"), sem("s1_ssq"), sem("s1_rsq")
        s_scaled, s_staged, s_sent = sem("s1_scaled"), sem("s1_staged"), [sem(f"s1_sent{i}") for i in range(SR)]
        s_zg, s_e, s_ln, s_tr, s_R, s_aug = (sem("s1_" + n) for n in ("zg", "e", "ln", "tr", "R", "aug"))

        def staged_wait(eng, u):
            if u >= SR:
                eng.wait_ge(s_sent[u % SR], 16 * (u // SR))

        with nc.Block() as block:
            @block.sync
            def _(sp):
                sp.dma_start(wb1[:], A["attn_norm_w"][0].partition_broadcast(P)).then_inc(s_wb, 16)
                for t in range(TT):
                    if t >= 2:
                        sp.wait_ge(s_xn, t - 1)
                    sp.dma_start(xin[:, t % 2, :], x2[tok(t), :]).then_inc(s_x[t % 2], 16)
                    if t == 1:
                        sp.wait_ge(s_zero, 1)
                        for r, c in ((0, C_FF), (32, C_MI), (64, C_MF)):
                            sp.dma_start(graw[:, :, r:r + H], w_in[:, :, c:c + H]).then_inc(s_gw, 16)
                        for r, n in ((0, "fox_f_bias"), (32, "mlstm_i_bias"), (64, "mlstm_f_bias")):
                            sp.dma_start(gb[r:r + H, :], A[n].rearrange("a h -> h a")).then_inc(s_gw, 16)
                        sp.dma_start(qkw[:, 0, :], A["fox_q_norm_w"][0].partition_broadcast(P)).then_inc(s_qkw, 16)
                        sp.dma_start(qkw[:, 1, :], A["fox_k_norm_w"][0].partition_broadcast(P)).then_inc(s_qkw, 16)
                        for n in (0, 1):
                            sp.dma_start(RAW[:, n], w_in[:, :, COLS[n]:COLS[n] + CH]).then_inc(s_raw[n], 16)
                for u in UNITS:
                    kind, j = STAGED[u]
                    n = u // TT
                    if j == 0 and 2 <= n + 1 < len(KINDS):
                        sp.wait_ge(s_w, n)
                        sp.dma_start(RAW[:, (n + 1) % 2], w_in[:, :, COLS[n + 1]:COLS[n + 1] + CH]).then_inc(s_raw[(n + 1) % 2], 16)
                    src = stage[:, u % SR].rearrange("p h c -> p (h c)")
                    if kind in ("q", "k"):
                        sp.wait_ge(s_scaled, u + 1)
                        sp.dma_start((dQ if kind == "q" else dK)[tok(j), :], src).then_inc(s_sent[u % SR], 16)
                    else:
                        sp.wait_ge(s_staged, u - 2 * TT + 1)
                        to = {"v": dV, "mv": dMV, "mo": dMO}
                        dst = to[kind][tok(j), :] if kind in to else dQK[tok(j // 2), (j % 2) * CH:(j % 2 + 1) * CH]
                        sp.dma_start(dst, src[:, 0:CH]).then_inc(s_sent[u % SR], 16)
                for i in range(SR):
                    sp.wait_ge(s_sent[i], 16 * len([u for u in UNITS if u % SR == i]))

            @block.gpsimd
            def _(pool):
                link = chain(pool, "s1_pool")
                pool.memset(graw[:], 0.0)
                pool.memset(gb[:], 0.0).then_inc(s_zero, 1)
                pool.memset(half[:], -0.5)
                pool.memset(onec[:], 1.0)
                pool.memset(ones[:], 1.0)
                pool.memset(before[:], 1.0)
                pool.memset(causal[:], 0.0)
                pool.memset(causalT[:], 0.0)
                pool.memset(ident[:], 0.0).then_inc(s_c, 1)
                pool.wait_ge(s_c, 1)
                pool.affine_select(out=ident[:], in_=ident[:], compare_op=ALU.not_equal, fill=1.0,
                                   base=0, pattern=[[-1, P]], channel_multiplier=1)
                pool.affine_select(out=before[:], in_=before[:], compare_op=ALU.is_gt, fill=0.0,
                                   base=0, pattern=[[1, P]], channel_multiplier=-1)
                pool.affine_select(out=causal[:], in_=causal[:], compare_op=ALU.is_ge, fill=NEG,
                                   base=0, pattern=[[-1, P]], channel_multiplier=1)
                pool.affine_select(out=causalT[:], in_=causalT[:], compare_op=ALU.is_ge, fill=NEG,
                                   base=0, pattern=[[1, P]], channel_multiplier=-1).then_inc(s_c, 1)
                for t in range(TT):
                    pool.wait_ge(s_ss, t + 1)
                    r = rmsA[:, t:t + 1]
                    inv_root(pool, link, r, r, D).then_inc(s_rstd, 1)
                pool.wait_ge(s_qkw, 32)
                pool.tensor_scalar(qkw[:, 0, :], qkw[:, 0, :], HD ** -0.5, None, ALU.mult).then_inc(s_c, 1)
                pool.wait_ge(s_c, 3)
                for u in range(2 * TT):
                    pool.wait_ge(s_ssq, u + 1)
                    if u >= 2:
                        pool.wait_ge(s_free["dve"], FREED[u][1])
                    inv_root(pool, link, rsq[:, u % 2], ssq[:, u % 2], HD).then_inc(s_rsq, 1)
                    pool.wait_ge(s_aug, u + 1)
                    v = stage[:, u % SR, :, 0:HD]
                    w = bc(qkw[:, u // TT, :].unsqueeze(1), [P, H, HD])
                    pool.tensor_tensor(v, v, w, ALU.mult).then_inc(s_scaled, 1)

            @block.scalar
            def _(act):
                link = chain(act, "s1_act")

                def split_hi(n):
                    act.wait_ge(s_raw[n % 2], 16 * (n // 2 + 1))
                    if n >= 2:
                        act.wait_ge(s_wused, n - 1)
                    act.activation(WH[:, n % 2], RAW[:, n % 2], ACT.Copy).then_inc(s_whi, 1)

                act.wait_ge(s_c, 2)
                for t in range(TT):
                    act.wait_ge(s_x[t % 2], 16 * (t // 2 + 1))
                    if t >= 1:
                        act.wait_ge(s_ss, t)
                    act.activation(sqr[:], xin[:, t % 2], ACT.Square, accum_out=rmsA[:, t:t + 1]).then_inc(s_ss, 1)
                    if t >= 1:
                        hi_of(act, t - 1, s_tp, s_hi, XH)
                hi_of(act, TT - 1, s_tp, s_hi, XH)
                act.wait_ge(s_gw, 96)
                act.activation(GH[:], graw[:], ACT.Copy).then_inc(s_ghi, 1)
                split_hi(0)
                split_hi(1)
                act.wait_ge(s_zg, 2)
                link(act.activation(lf[:], zg[:], ACT.Abs))
                link(act.activation(lf[:], lf[:], ACT.Exp, scale=-1.0))
                act.activation(lf[:], lf[:], ACT.Ln, bias=onec[:, 0:1]).then_inc(s_ln, 1)
                for b in range(2):
                    act.wait_ge(s_tr, b + 1)
                    act.activation(TR[:, 4 * b:4 * b + 4, :].rearrange("p t c -> p (t c)"), ps[b][:], ACT.Copy).then_inc(s_e, 1)
                for u in UNITS:
                    kind, j = STAGED[u]
                    n, o = u // TT, u + 2
                    b = ps[2 + o % RING]
                    if j == 2 and 1 <= n < len(KINDS) - 1:
                        split_hi(n + 1)
                    act.wait_ge(s_out, o + 1)
                    if kind in ("q", "k"):
                        if u >= 1:
                            act.wait_ge(s_ssq, u)
                        act.activation(sq[:], b[:], ACT.Square).then_inc(s_sq, 1)
                    else:
                        staged_wait(act, u)
                        fn = ACT.Sigmoid if kind == "mo" else ACT.Copy
                        dst = stage[:, u % SR].rearrange("p h c -> p (h c)")[:, 0:CH]
                        ins = act.activation(dst, b[:], fn)
                        ins.then_inc(s_free["act"], 1)
                        act.wait_ge(s_free["act"], FREED[o][1])
                        act.sem_inc(s_staged, 1)

            @block.vector
            def _(dve):
                link = chain(dve, "s1_dve")

                def split_lo(n):
                    dve.wait_ge(s_whi, n + 1)
                    dve.tensor_tensor(WL[:, n % 2], RAW[:, n % 2], WH[:, n % 2].bitcast(f32), ALU.subtract).then_inc(s_w, 1)

                dve.wait_ge(s_wb, 16)
                for t in range(TT):
                    dve.wait_ge(s_rstd, t + 1)
                    if t >= 2:
                        dve.wait_ge(s_tp, t - 1)
                    dve.scalar_tensor_tensor(out=xn[:, t % 2], in0=xin[:, t % 2], scalar=rmsA[:, t:t + 1], in1=wb1[:],
                                             op0=ALU.mult, op1=ALU.mult).then_inc(s_xn, 1)
                    if t >= 1:
                        lo_of(dve, t - 1, s_hi, s_hT, XH, XL)
                lo_of(dve, TT - 1, s_hi, s_hT, XH, XL)
                dve.wait_ge(s_ghi, 1)
                dve.tensor_tensor(GL[:], graw[:], GH[:].bitcast(f32), ALU.subtract).then_inc(s_g, 1)
                split_lo(0)
                dve.wait_ge(s_g, 1)
                split_lo(1)
                for o in (0, 1):
                    dve.wait_ge(s_out, o + 1)
                    if o == 0:
                        dve.wait_ge(s_hT, TT)
                    dve.tensor_scalar(zg[:, o * CH:(o + 1) * CH], ps[2 + o][:], gb[:, 0:1], None, ALU.add).then_inc(s_zg, 1)
                    dve.wait_ge(s_zg, o + 1)
                    dve.sem_inc(s_free["dve"], 1)
                dve.wait_ge(s_ln, 1)
                link(dve.scalar_tensor_tensor(out=lf[:], in0=zg[:], scalar=0.0, in1=lf[:], op0=ALU.min, op1=ALU.subtract))
                link(dve.memset(gt[:], 1.0))
                link(dve.tensor_tensor_scan(cum[:], gt[:], lf[:], 0.0, ALU.mult, ALU.add))
                link(dve.memset(R[:], 0.0))
                link(dve.tensor_copy(R[0:H], cum[0:H]))
                link(dve.tensor_copy(gt[32:32 + H], cum[64:64 + H]))
                link(dve.tensor_tensor(R[32:32 + H], zg[32:32 + H], gt[32:32 + H], ALU.subtract))
                link(dve.tensor_tensor_scan(gt[32:32 + H], R[32:32 + H], R[32:32 + H], 0.0, ALU.max, ALU.max))
                link(dve.tensor_copy(R[64:64 + H], gt[32:32 + H]))
                link(dve.tensor_tensor(gt[64:64 + H], R[64:64 + H], cum[64:64 + H], ALU.add))
                link(dve.tensor_copy(R[96:96 + H], gt[64:64 + H]))
                dve.sem_inc(s_R, 1)
                dve.wait_ge(s_e, 2)
                for u in UNITS:
                    kind, j = STAGED[u]
                    n, o = u // TT, u + 2
                    b = ps[2 + o % RING]
                    if j == 2 and 1 <= n < len(KINDS) - 1:
                        split_lo(n + 1)
                    if kind not in ("q", "k"):
                        continue
                    dve.wait_ge(s_sq, u + 1)
                    if u >= 2:
                        dve.wait_ge(s_rsq, u - 1)
                    dve.tensor_reduce(ssq[:, u % 2], sq[:].rearrange("p (h c) -> p h c", h=H), X, ALU.add).then_inc(s_ssq, 1)
                    staged_wait(dve, u)
                    a, c = (HD, HD + 1) if kind == "q" else (HD + 1, HD)
                    dve.tensor_scalar(stage[:, u % SR, :, a:a + 1], TR[:, j, 0:H].unsqueeze(2), 1.0 if kind == "q" else -1.0, None, ALU.mult)
                    dve.memset(stage[:, u % SR, :, c:c + 1], 1.0)
                    dve.wait_ge(s_rsq, u + 1)
                    r = bc(rsq[:, u % 2].unsqueeze(2), [P, H, HD])
                    dve.tensor_tensor(stage[:, u % SR, :, 0:HD], b[:].rearrange("p (h c) -> p h c", h=H), r, ALU.mult).then_inc(s_free["dve"], 1)
                    dve.wait_ge(s_free["dve"], FREED[o][1])
                    dve.sem_inc(s_aug, 1)

            @block.tensor
            def _(pe):
                pe.wait_ge(s_c, 2)
                for t in range(TT):
                    pe.wait_ge(s_xn, t + 1)
                    transposes_of(pe, t, xn[:, t % 2], s_hT, s_tp)
                pe.wait_ge(s_hT, TT)
                pe.wait_ge(s_g, 1)
                for hf in range(2):
                    cols = slice(hf * CH, (hf + 1) * CH)
                    for k in range(KT):
                        last = mm3(pe, ps[2 + hf][:], GH[:, k], GL[:, k], XH[:, k, cols], XL[:, k, cols], k == 0, k == KT - 1)
                    last.then_inc(s_out, 1)
                for u in UNITS:
                    kind, j = STAGED[u]
                    n, o = u // TT, u + 2
                    if u == 2:
                        pe.wait_ge(s_R, 1)
                        for b in range(2):
                            for i in range(4):
                                last = pe.transpose(ps[b][:, i * P:(i + 1) * P], R[:, tok(4 * b + i)], ident[:])
                            last.then_inc(s_tr, 1)
                    if j == 0:
                        pe.wait_ge(s_w, n + 1)
                    if o >= RING:
                        e, c = FREED[o - RING]
                        pe.wait_ge(s_free[e], c)
                    b = ps[2 + o % RING]
                    for k in range(KT):
                        if kind == "qk":
                            c, cols = tok(j // 2), slice((j % 2) * CH, (j % 2 + 1) * CH)
                            last = mm3(pe, b[:], WH[:, n % 2, k, c], WL[:, n % 2, k, c], XH[:, k, cols], XL[:, k, cols], k == 0, k == KT - 1)
                        else:
                            last = mm3(pe, b[:], XH[:, k, tok(j)], XL[:, k, tok(j)], WH[:, n % 2, k], WL[:, n % 2, k], k == 0, k == KT - 1)
                    last.then_inc(s_out, 1)
                    if j == TT - 1:
                        pe.wait_ge(s_out, o + 1)
                        pe.sem_inc(s_wused, 1)

    def transposes_of(pe, t, src, s_free, s_done):
        if t >= 2:
            pe.wait_ge(s_free, t - 1)
        for g in range(2):
            b = ps[2 * (t % 2) + g]
            for i in range(4):
                last = pe.transpose(b[:, i * P:(i + 1) * P], src[:, (4 * g + i) * P:(4 * g + i + 1) * P], ident[:])
        last.then_inc(s_done, 1)

    def hi_of(act, t, s_done, s_hi, to):
        act.wait_ge(s_done, t + 1)
        for g in range(2):
            ins = act.activation(to[:, 4 * g:4 * g + 4, tok(t)], ps[2 * (t % 2) + g][:].rearrange("p (k c) -> p k c", k=4), ACT.Copy)
        ins.then_inc(s_hi, 1)

    def lo_of(dve, t, s_hi, s_done, hi, lo):
        dve.wait_ge(s_hi, t + 1)
        for g in range(2):
            ins = dve.tensor_tensor(lo[:, 4 * g:4 * g + 4, tok(t)], ps[2 * (t % 2) + g][:].rearrange("p (k c) -> p k c", k=4),
                                    hi[:, 4 * g:4 * g + 4, tok(t)].bitcast(f32), ALU.subtract)
        ins.then_inc(s_done, 1)

    r2 = Region(A_X, 128 * KB)
    U = r2.take("U", [P, 4, S + 3])
    CV = r2.take("CV", [P, 4, S])
    SG = r2.take("SG", [P, 4, S])
    QKT = r2.take("QKT", [P, 4, S])
    VAU = r2.take("VAU", [P, TT, H, VA])
    KTOK = r2.take("KTOK", [P, TT, 2 * P])
    SELA = r2.take("SELA", [P, H, P])
    SELM = r2.take("SELM", [P, H, P])
    last_row = r2.take("last_row", [P, P])
    QZ = r2.take("QZ", [P, 2, H, P])
    r2r = Region(A_RAW, 32 * KB)
    MY = r2r.take("MY", [P, TT, CH])
    MOS = r2r.take("MOS", [P, 2, CH])
    mow = r2r.take("mow", [P, CH])
    WT = r2r.take("WT", [P, H, P])
    CST = r2r.take("CST", [P, 2, 4 * VA])
    kw = r2r.take("kw", [P, 2 * P])
    r2e = Region(E0, left - (E0 - A_E))
    PT = r2e.take("PT", [P, H, P])
    num = r2e.take("num", [P, H, VA])
    tmp = r2e.take("tmp", [P, H, VA])
    yh = r2e.take("yh", [P, 2, H, HD])
    ysq = r2e.take("ysq", [P, CH])
    MB = r2e.take("MB", [P, TT + 1, H])
    ex = r2e.take("ex", [P, 4, TT, H])
    cw = r2e.take("cw", [P, 4, 4])
    den = r2e.take("den", [P, 2, H])
    ysum = r2e.take("ysum", [P, 2, H])

    def stage2():
        def s2(n):
            return sem("s2_" + n)
        s_u, s_cw, s_v, s_w, s_mo = s2("u"), s2("convw"), s2("values"), s2("outw"), [s2("mo0"), s2("mo1")]
        s_qzero, s_qz, s_uz, s_sel, s_vone = s2("qzero"), s2("qz"), s2("uz"), s2("sel"), s2("vone")
        s_cv, s_sg, s_qk, s_kt, s_ktok = s2("conv"), s2("sig"), s2("qkt"), s2("kt"), s2("ktok")
        s_mb, s_mbs, s_exin, s_ex = s2("mb"), s2("mbs"), s2("exin"), s2("ex")
        s_D, s_S, s_int, s_Dm, s_WT, s_PT = s2("D"), s2("S"), s2("inter"), s2("Dmasked"), s2("WT"), s2("PT")
        s_tmp, s_kw, s_intra, s_num, s_upd, s_C = s2("tmp"), s2("kw"), s2("intra"), s2("num"), s2("upd"), s2("C")
        s_y, s_ysq, s_ysum, s_rs, s_done, s_mow = s2("y"), s2("ysq"), s2("ysum"), s2("rs"), s2("done"), s2("mow")

        with nc.Block() as block:
            @block.sync
            def _(sp):
                for j in range(4):
                    sp.dma_start(cw[:, j], A["mlstm_conv_w"][0, j].rearrange("(c p) -> p c", p=P), allow_slow_non_contiguous=True).then_inc(s_cw, 16)
                sp.dma_start(U[:, :, 3:S + 3], dQK.rearrange("(c p) s -> p c s", p=P)).then_inc(s_u, 16)
                sp.dma_start(mow[:], A["mlstm_out_norm_w"][0].partition_broadcast(P)).then_inc(s_w, 16)
                for t in range(TT):
                    sp.dma_start(VAU[:, t, :, 0:HD], dMV[tok(t), :].rearrange("p (h d) -> p h d", h=H)).then_inc(s_v, 16)
                for t in range(TT):
                    if t >= 2:
                        sp.wait_ge(s_mow, t - 1)
                    sp.dma_start(MOS[:, t % 2], dMO[tok(t), :]).then_inc(s_mo[t % 2], 16)

            @block.gpsimd
            def _(pool):
                link = chain(pool, "s2_pool")
                pool.memset(U[:, :, 0:3], 0.0).then_inc(s_uz, 1)
                pool.memset(SELA[:], 0.0)
                pool.memset(SELM[:], 0.0)
                link(pool.memset(last_row[:], 0.0))
                pool.memset(CST[:], 0.0)
                pool.affine_select(out=last_row[:], in_=last_row[:], compare_op=ALU.not_equal, fill=1.0,
                                   base=1 - P, pattern=[[0, P]], channel_multiplier=1).then_inc(s_sel, 1)
                pool.affine_select(out=SELA[:], in_=SELA[:], compare_op=ALU.not_equal, fill=1.0,
                                   base=-32, pattern=[[-1, H], [0, P]], channel_multiplier=1)
                pool.affine_select(out=SELM[:], in_=SELM[:], compare_op=ALU.not_equal, fill=-1.0,
                                   base=-64, pattern=[[-1, H], [0, P]], channel_multiplier=1).then_inc(s_sel, 1)
                pool.memset(VAU[:, :, :, HD:VA], 1.0).then_inc(s_vone, 1)
                pool.memset(QZ[:], 0.0).then_inc(s_qzero, 1)
                pool.wait_ge(s_ktok, 4)
                pool.wait_ge(s_ex, 1)
                pool.wait_ge(s_w, 16)

                def finish(t):
                    pool.wait_ge(s_mo[t % 2], 16 * (t // 2 + 1))
                    pool.tensor_tensor(MOS[:, t % 2], MOS[:, t % 2], mow[:], ALU.mult).then_inc(s_rs, 1)
                    pool.wait_ge(s_ysum, t + 1)
                    link(inv_root(pool, link, ysum[:, t % 2], ysum[:, t % 2], HD))
                    pool.wait_ge(s_ysq, t + 1)
                    pool.wait_ge(s_rs, t + 1)
                    y = yh[:, t % 2]
                    link(pool.tensor_tensor(y, y, bc(ysum[:, t % 2].unsqueeze(2), [P, H, HD]), ALU.mult))
                    pool.tensor_tensor(MY[:, t], y.rearrange("p h d -> p (h d)"), MOS[:, t % 2], ALU.mult).then_inc(s_mow, 1)

                for t in range(TT):
                    if t >= 1:
                        pool.wait_ge(s_upd, t)
                    k = kw[:].rearrange("p (h d) -> p h d", h=H)
                    pool.tensor_tensor(k, KTOK[:, t].rearrange("p (h d) -> p h d", h=H),
                                       bc(ex[:, 1, t].unsqueeze(2), [P, H, QK]), ALU.mult).then_inc(s_kw, 1)
                    if t >= 1:
                        finish(t - 1)
                finish(TT - 1)

            @block.scalar
            def _(act):
                for c in range(4):
                    act.wait_ge(s_cv, c + 1)
                    act.activation(SG[:, c], CV[:, c], ACT.Sigmoid).then_inc(s_sg, 1)
                def spread(t):
                    if t >= 2:
                        act.wait_ge(s_S, t - 1)
                    for h in range(H):
                        rows = slice(32 * (h % 4), 32 * (h % 4) + 32)
                        last = act.activation(QZ[rows, t % 2, h], QKT[rows, h // 4, tok(t)], ACT.Copy)
                    last.then_inc(s_qz, 1)

                act.wait_ge(s_qk, 2)
                act.wait_ge(s_qzero, 1)
                spread(0)
                for i in range(4):
                    act.wait_ge(s_kt, i + 1)
                    act.activation(KTOK[:, 4 * (i % 2):4 * (i % 2) + 4, (i // 2) * P:(i // 2 + 1) * P],
                                   ps[4 + i][:].rearrange("p (t c) -> p t c", t=4), ACT.Copy).then_inc(s_ktok, 1)
                act.wait_ge(s_exin, 1)
                act.activation(ex[:], ex[:], ACT.Exp).then_inc(s_ex, 1)
                for t in range(TT + 1):
                    if t < TT:
                        act.wait_ge(s_Dm, t + 1)
                        act.activation(WT[:], WT[:], ACT.Exp).then_inc(s_WT, 1)
                        if t + 1 < TT:
                            spread(t + 1)
                    if t >= 1:
                        act.wait_ge(s_y, t)
                        if t >= 2:
                            act.wait_ge(s_ysum, t - 1)
                        act.activation(ysq[:], yh[:, (t - 1) % 2].rearrange("p h d -> p (h d)"), ACT.Square).then_inc(s_ysq, 1)

            @block.vector
            def _(dve):
                link = chain(dve, "s2_dve")
                dve.wait_ge(s_cw, 64)
                dve.wait_ge(s_u, 16)
                dve.wait_ge(s_uz, 1)
                for c in range(4):
                    link(dve.tensor_scalar(CV[:, c], U[:, c, 3:S + 3], cw[:, 3, c:c + 1], None, ALU.mult))
                    for j in (2, 1):
                        link(dve.scalar_tensor_tensor(out=CV[:, c], in0=U[:, c, j:j + S], scalar=cw[:, j, c:c + 1], in1=CV[:, c], op0=ALU.mult, op1=ALU.add))
                    dve.scalar_tensor_tensor(out=CV[:, c], in0=U[:, c, 0:S], scalar=cw[:, 0, c:c + 1], in1=CV[:, c],
                                             op0=ALU.mult, op1=ALU.add).then_inc(s_cv, 1)
                dve.wait_ge(s_mb, 1)
                dve.memset(MB[:, 0], 0.0)
                link(dve.tensor_copy(MB[:, 1:], ps[0][:, 0:TT * H].rearrange("p (t h) -> p t h", t=TT)))
                dve.tensor_tensor(ex[:, 0], MB[:, 0:TT], TR[:, :, 64:64 + H], ALU.subtract)
                dve.tensor_tensor(ex[:, 1], TR[:, :, 32:32 + H], MB[:, 1:], ALU.subtract)
                dve.tensor_tensor(ex[:, 2], MB[:, 0:TT], MB[:, 1:], ALU.subtract)
                dve.tensor_scalar(ex[:, 3], TR[:, :, 96:96 + H], -1.0, None, ALU.mult).then_inc(s_exin, 1)
                for c in range(4):
                    dve.wait_ge(s_sg, c + 1)
                    dve.scalar_tensor_tensor(out=QKT[:, c], in0=CV[:, c], scalar=1.0 if c < 2 else QK ** -0.5, in1=SG[:, c],
                                             op0=ALU.mult, op1=ALU.mult).then_inc(s_qk, 1)
                dve.wait_ge(s_ex, 1)

                def mask(t):
                    dve.wait_ge(s_D, t + 1)
                    if t >= 1:
                        dve.wait_ge(s_PT, t)
                    for g in range(2):
                        last = dve.scalar_tensor_tensor(out=WT[:, 4 * g:4 * g + 4], in0=ps[g][:].rearrange("p (h c) -> p h c", h=4), scalar=0.0,
                                                        in1=bc(causalT[:].unsqueeze(1), [P, 4, P]), op0=ALU.min, op1=ALU.add)
                    last.then_inc(s_Dm, 1)

                def squares(t):
                    dve.wait_ge(s_ysq, t + 1)
                    dve.tensor_reduce(ysum[:, t % 2], ysq[:].rearrange("p (h c) -> p h c", h=H), X, ALU.add).then_inc(s_ysum, 1)

                mask(0)
                for t in range(TT):
                    dve.wait_ge(s_S, t + 1)
                    dve.wait_ge(s_WT, t + 1)
                    if t >= 1:
                        dve.wait_ge(s_intra, t)
                    for g in range(2):
                        last = dve.tensor_tensor(PT[:, 4 * g:4 * g + 4], ps[2 + g][:].rearrange("p (h c) -> p h c", h=4), WT[:, 4 * g:4 * g + 4], ALU.mult)
                    last.then_inc(s_PT, 1)
                    dve.wait_ge(s_int, t + 1)
                    for g in range(2):
                        last = dve.tensor_tensor(tmp[:, 4 * g:4 * g + 4], ps[4 + g][:, 0:4 * VA].rearrange("p (h c) -> p h c", h=4),
                                                 bc(ex[:, 0, t, 4 * g:4 * g + 4].unsqueeze(2), [P, 4, VA]), ALU.mult)
                    last.then_inc(s_tmp, 1)
                    if t >= 1:
                        squares(t - 1)
                    dve.wait_ge(s_tmp, t + 1)
                    dve.wait_ge(s_intra, t + 1)
                    for g in range(2):
                        last = dve.tensor_tensor(num[:, 4 * g:4 * g + 4], tmp[:, 4 * g:4 * g + 4], ps[6 + g][:, 0:4 * VA].rearrange("p (h c) -> p h c", h=4), ALU.add)
                    last.then_inc(s_num, 1)
                    if t + 1 < TT:
                        mask(t + 1)
                    dve.wait_ge(s_upd, t + 1)
                    for h in range(H):
                        j, g = h % 4, h // 4
                        rows, cols = slice(32 * j, 32 * j + 32), slice(j * VA, (j + 1) * VA)
                        last = dve.scalar_tensor_tensor(out=CST[rows, g, cols], in0=CST[rows, g, cols], scalar=ex[rows, 2, t, h:h + 1],
                                                        in1=ps[4 + g][rows, cols], op0=ALU.mult, op1=ALU.add)
                    last.then_inc(s_C, 1)
                    dve.wait_ge(s_num, t + 1)
                    d = den[:, t % 2]
                    link(dve.tensor_tensor(d.unsqueeze(2), num[:, :, HD:VA], ex[:, 3, t].unsqueeze(2), ALU.max))
                    link(dve.scalar_tensor_tensor(out=d.unsqueeze(2), in0=num[:, :, HD:VA], scalar=-1.0, in1=d.unsqueeze(2), op0=ALU.mult, op1=ALU.max))
                    link(dve.reciprocal(d, d))
                    if t >= 2:
                        dve.wait_ge(s_mow, t - 1)
                    dve.tensor_tensor(yh[:, t % 2], num[:, :, 0:HD], bc(d.unsqueeze(2), [P, H, HD]), ALU.mult).then_inc(s_y, 1)
                    dve.wait_ge(s_y, t + 1)
                    dve.wait_ge(s_C, t + 1)
                squares(TT - 1)

            @block.tensor
            def _(pe):
                pe.wait_ge(s_sel, 1)
                pe.matmul(ps[0][:, 0:TT * H], last_row[:], TR[:, :, 64:64 + H], start=True, stop=True).then_inc(s_mb, 1)
                pe.wait_ge(s_qk, 4)
                for i in range(4):
                    c = 2 + i // 2
                    for n in range(4):
                        last = pe.transpose(ps[4 + i][:, n * P:(n + 1) * P], QKT[:, c, tok(4 * (i % 2) + n)], ident[:])
                    last.then_inc(s_kt, 1)
                pe.wait_ge(s_sel, 2)
                pe.wait_ge(s_exin, 1)

                def decays(t):
                    if t >= 1:
                        pe.wait_ge(s_Dm, t)
                    for h in range(H):
                        o = ps[h // 4][:, (h % 4) * P:(h % 4 + 1) * P]
                        pe.matmul(o, R[:, tok(t)], SELA[:, h], start=True, stop=False)
                        last = pe.matmul(o, SELM[:, h], R[:, tok(t)], start=False, stop=True)
                    last.then_inc(s_D, 1)

                def scores(t):
                    if t >= 1:
                        pe.wait_ge(s_PT, t)
                    pe.wait_ge(s_qz, t + 1)
                    for g in range(2):
                        last = pe.matmul(ps[2 + g][:], QKT[:, 2 + g, tok(t)], QZ[:, t % 2, 4 * g:4 * g + 4].rearrange("p h c -> p (h c)"), start=True, stop=True)
                    last.then_inc(s_S, 1)

                decays(0)
                scores(0)
                pe.wait_ge(s_vone, 1)
                pe.wait_ge(s_v, 16 * TT)
                pe.wait_ge(s_ktok, 4)
                for t in range(TT):
                    if t + 1 < TT:
                        decays(t + 1)
                    if t >= 1:
                        pe.wait_ge(s_C, t)
                    for g in range(2):
                        last = pe.matmul(ps[4 + g][:, 0:4 * VA], QKT[:, g, tok(t)], CST[:, g], start=True, stop=True)
                    last.then_inc(s_int, 1)
                    pe.wait_ge(s_PT, t + 1)
                    if t >= 1:
                        pe.wait_ge(s_num, t)
                    for h in range(H):
                        last = pe.matmul(ps[6 + h // 4][:, (h % 4) * VA:(h % 4 + 1) * VA], PT[:, h], VAU[:, t, h], start=True, stop=True)
                    last.then_inc(s_intra, 1)
                    if t + 1 < TT:
                        scores(t + 1)
                    pe.wait_ge(s_kw, t + 1)
                    pe.wait_ge(s_tmp, t + 1)
                    for g in range(2):
                        last = pe.matmul(ps[4 + g][:, 0:4 * VA], kw[:, g * P:(g + 1) * P], VAU[:, t, 4 * g:4 * g + 4].rearrange("p h c -> p (h c)"), start=True, stop=True)
                    last.then_inc(s_upd, 1)

    r3w = Region(A_W, 64 * KB)
    KTT = r3w.take("KTT", [P, H, S])
    VS = r3w.take("VS", [P, TT, CH])
    PB = r3w.take("PB", [P, 2, S])
    PTS = r3w.take("PTS", [P, 2, TT, P])
    QTT = Region(A_RAW + 16 * KB, 32 * KB).take("QTT", [P, H, S])
    r3e = Region(E0, left - (E0 - A_E))
    qks = r3e.take("qks", [P, 2, H * AUG])
    mixf = r3e.take("mixf", [P, 2, CH])
    fsq = r3e.take("fsq", [P, CH])
    fw = r3e.take("fw", [P, CH])
    zeros = r3e.take("zeros", [P, CH])
    nmax = r3e.take("nmax", [P, 2])
    rowsum = r3e.take("rowsum", [P, 2, H])
    fsum = r3e.take("fsum", [P, 2, H])
    NU = TT * H
    USERS, MIXAT = [], 4
    for u_ in range(NU):
        USERS.append(("p", u_))
        if u_ >= H and u_ % H == MIXAT:
            USERS.append(("m", u_ // H - 1))
    USERS.append(("m", TT - 1))
    USER_OF = {x: i for i, x in enumerate(USERS)}
    ACT_OUT = []
    for kind_, i_ in USERS:
        ACT_OUT.append((ACT_OUT[-1] if ACT_OUT else 0) + (1 if kind_ == "p" and i_ // H >= 4 else 0))

    def stage3():
        def s3(n):
            return sem("s3_" + n)
        s_ld = [s3("ld0"), s3("ld1")]
        s_v, s_fw, s_qkt = s3("values"), s3("outw"), s3("qkt")
        s_ka, s_kd = s3("out_act"), s3("out_dve")
        s_S, s_msk, s_nmax, s_P, s_T, s_ptd, s_pta = s3("S"), s3("masked"), s3("nmax"), s3("P"), s3("T"), s3("pt_dve"), s3("pt_act")
        s_pv, s_o, s_fsq, s_fsum, s_mix, s_hi = s3("pv"), s3("o"), s3("fsq"), s3("fsum"), s3("mix"), s3("hi")
        s_ri, s_zero, s_filled = s3("ri"), s3("zero"), s3("filled")

        with nc.Block() as block:
            @block.sync
            def _(sp):
                for i in range(2 * TT):
                    if i >= 2:
                        sp.wait_ge(s_qkt, i - 1)
                    src = dK if i < TT else dQ
                    sp.dma_start(qks[:, i % 2], src[tok(i % TT), :]).then_inc(s_ld[i % 2], 16)
                sp.dma_start(VS[:], dV.rearrange("(t p) c -> p t c", p=P)).then_inc(s_v, 16)
                sp.dma_start(fw[:], A["fox_out_norm_w"][0].partition_broadcast(P)).then_inc(s_fw, 16)
                sp.wait_ge(s_zero, 1)
                for b in range(S * TOPK // P, SBMAX):
                    sp.dma_start(dY[b * P:(b + 1) * P, :].rearrange("p (a c) -> p a c", a=2), bc(zeros[:].unsqueeze(1), [P, 2, CH])).then_inc(s_filled, 16)
                sp.wait_ge(s_filled, 16 * (SBMAX - S * TOPK // P))

            @block.gpsimd
            def _(pool):
                link = chain(pool, "s3_pool")
                pool.memset(zeros[:], 0.0).then_inc(s_zero, 1)
                pool.wait_ge(s_fw, 16)
                for t in range(TT):
                    pool.wait_ge(s_fsum, t + 1)
                    link(inv_root(pool, link, fsum[:, t % 2], fsum[:, t % 2], HD))
                    y = mixf[:, t % 2]
                    yv = y.rearrange("p (h d) -> p h d", h=H)
                    link(pool.tensor_tensor(yv, yv, bc(fsum[:, t % 2].unsqueeze(2), [P, H, HD]), ALU.mult))
                    pool.tensor_tensor(y, y, fw[:], ALU.mult).then_inc(s_mix, 1)

            @block.scalar
            def _(act):
                for i in range(2 * TT):
                    act.wait_ge(s_qkt, i + 1)
                    to = KTT if i < TT else QTT
                    act.activation(to[0:AUG, 0:4, tok(i % TT)], ps[2 * (i % 2)][0:AUG].rearrange("p (h c) -> p h c", h=4), ACT.Copy).then_inc(s_ka, 1)

                def after(u):
                    t, h = u // H, u % H
                    if t >= 4:
                        act.wait_ge(s_T, USER_OF["p", u] + 1)
                        if u >= 2:
                            act.wait_ge(s_pv, u - 1)
                        act.activation(PTS[:, u % 2, 4:t + 1], ps[5][:, 0:(t - 3) * P].rearrange("p (t c) -> p t c", c=P), ACT.Copy).then_inc(s_pta, 1)
                    if u >= H and h == MIXAT:
                        mixed(t - 1)

                def mixed(t):
                    act.wait_ge(s_T, USER_OF["m", t] + 1)
                    for g in range(2):
                        last = act.activation(XH[:, 4 * g:4 * g + 4, tok(t)], ps[4 + g][:].rearrange("p (k c) -> p k c", k=4), ACT.Copy)
                    last.then_inc(s_hi, 1)

                for u in range(NU):
                    t, h = u // H, u % H
                    act.wait_ge(s_nmax, u + 1)
                    if u >= 2:
                        act.wait_ge(s_T, USER_OF["p", u - 2] + 1)
                    if t >= 2 and h == 0:
                        act.wait_ge(s_o, t - 1)
                    if t < 4:
                        act.activation(PB[:, u % 2, 0:(t + 1) * P], ps[2 * (u % 2)][:, 0:(t + 1) * P], ACT.Exp, bias=nmax[:, u % 2:u % 2 + 1],
                                       accum_out=rowsum[:, t % 2, h:h + 1]).then_inc(s_P, 1)
                    else:
                        act.activation(PB[:, u % 2, 0:(t + 1) * P], pair(u % 2, (t + 1) * P), ACT.Exp, bias=nmax[:, u % 2:u % 2 + 1],
                                       accum_out=rowsum[:, t % 2, h:h + 1]).then_inc(s_P, 1)
                    if u >= 1:
                        after(u - 1)
                    if h == 2 and t >= 1:
                        act.wait_ge(s_o, t)
                        if t >= 2:
                            act.wait_ge(s_fsum, t - 1)
                        act.activation(fsq[:], mixf[:, (t - 1) % 2], ACT.Square).then_inc(s_fsq, 1)
                after(NU - 1)
                act.wait_ge(s_o, TT)
                act.wait_ge(s_fsum, TT - 1)
                act.activation(fsq[:], mixf[:, (TT - 1) % 2], ACT.Square).then_inc(s_fsq, 1)
                mixed(TT - 1)

            @block.vector
            def _(dve):
                for i in range(2 * TT):
                    dve.wait_ge(s_qkt, i + 1)
                    to = KTT if i < TT else QTT
                    dve.tensor_copy(to[0:AUG, 4:8, tok(i % TT)], ps[2 * (i % 2) + 1][0:AUG].rearrange("p (h c) -> p h c", h=4)).then_inc(s_kd, 1)

                def after(u):
                    t, h = u // H, u % H
                    dve.wait_ge(s_T, USER_OF["p", u] + 1)
                    if u >= 2:
                        dve.wait_ge(s_pv, u - 1)
                    n = min(t + 1, 4)
                    dve.tensor_copy(PTS[:, u % 2, 0:n], ps[4][:, 0:n * P].rearrange("p (t c) -> p t c", c=P)).then_inc(s_ptd, 1)
                    if u >= H and h == MIXAT:
                        mixed(t - 1)

                def mixed(t):
                    dve.wait_ge(s_hi, t + 1)
                    for g in range(2):
                        last = dve.tensor_tensor(XL[:, 4 * g:4 * g + 4, tok(t)], ps[4 + g][:].rearrange("p (k c) -> p k c", k=4),
                                                 XH[:, 4 * g:4 * g + 4, tok(t)].bitcast(f32), ALU.subtract)
                    last.then_inc(s_ptd, 1)

                def outputs(t):
                    dve.wait_ge(s_pv, H * (t + 1))
                    dve.reciprocal(rowsum[:, t % 2], rowsum[:, t % 2]).then_inc(s_ri, 1)
                    dve.wait_ge(s_ri, t + 1)
                    if t >= 2:
                        dve.wait_ge(s_T, USER_OF["m", t - 2] + 1)
                    dve.tensor_tensor(mixf[:, t % 2].rearrange("p (h d) -> p h d", h=H), ps[6 + t % 2][:].rearrange("p (h d) -> p h d", h=H),
                                      bc(rowsum[:, t % 2].unsqueeze(2), [P, H, HD]), ALU.mult).then_inc(s_o, 1)

                def squares(t):
                    dve.wait_ge(s_fsq, t + 1)
                    dve.tensor_reduce(fsum[:, t % 2], fsq[:].rearrange("p (h c) -> p h c", h=H), X, ALU.add).then_inc(s_fsum, 1)

                for u in range(NU):
                    t, h = u // H, u % H
                    n = (t + 1) * P
                    dve.wait_ge(s_S, u + 1)
                    d = ps[2 * (u % 2) + (t // 4)][:, (t % 4) * P:(t % 4 + 1) * P]
                    dve.tensor_tensor(d, d, causal[:], ALU.add).then_inc(s_msk, 1)
                    dve.wait_ge(s_msk, u + 1)
                    if u >= 2:
                        dve.wait_ge(s_P, u - 1)
                    dve.tensor_reduce(nmax[:, u % 2:u % 2 + 1], pair(u % 2, n), X, ALU.max, negate=True).then_inc(s_nmax, 1)
                    if u >= 1:
                        after(u - 1)
                    if h == 1 and t >= 1:
                        outputs(t - 1)
                    if h == 3 and t >= 1:
                        squares(t - 1)
                after(NU - 1)
                outputs(TT - 1)
                squares(TT - 1)
                mixed(TT - 1)

            @block.tensor
            def _(pe):
                for i in range(2 * TT):
                    pe.wait_ge(s_ld[i % 2], 16 * (i // 2 + 1))
                    if i >= 2:
                        pe.wait_ge(s_ka, i - 1)
                        pe.wait_ge(s_kd, i - 1)
                    for h in range(H):
                        last = pe.transpose(ps[2 * (i % 2) + h // 4][0:AUG, (h % 4) * P:(h % 4 + 1) * P], qks[:, i % 2, h * AUG:(h + 1) * AUG], ident[:])
                    last.then_inc(s_qkt, 1)
                pe.wait_ge(s_ka, 2 * TT)
                pe.wait_ge(s_kd, 2 * TT)

                def scores(u):
                    t, h = u // H, u % H
                    if u >= 2:
                        pe.wait_ge(s_P, u - 1)
                    for g in range(t // 4 + 1):
                        n = min((t + 1) * P - g * CH, CH)
                        last = pe.matmul(ps[2 * (u % 2) + g][:, 0:n], QTT[0:AUG, h, tok(t)], KTT[0:AUG, h, g * CH:g * CH + n], start=True, stop=True)
                    last.then_inc(s_S, 1)

                def free_banks(i):
                    if i >= 1:
                        pe.wait_ge(s_ptd, i)
                        if ACT_OUT[i - 1]:
                            pe.wait_ge(s_pta, ACT_OUT[i - 1])

                def turn(u):
                    t = u // H
                    pe.wait_ge(s_P, u + 1)
                    free_banks(USER_OF["p", u])
                    for j in range(t + 1):
                        last = pe.transpose(ps[4 + j // 4][:, (j % 4) * P:(j % 4 + 1) * P], PB[:, u % 2, j * P:(j + 1) * P], ident[:])
                    last.then_inc(s_T, 1)
                    if u >= H and u % H == MIXAT:
                        mixed(t - 1)

                def mixed(t):
                    pe.wait_ge(s_mix, t + 1)
                    free_banks(USER_OF["m", t])
                    for k in range(KT):
                        src = mixf[:, t % 2, k * P:(k + 1) * P] if k < 4 else MY[:, t, (k - 4) * P:(k - 3) * P]
                        last = pe.transpose(ps[4 + k // 4][:, (k % 4) * P:(k % 4 + 1) * P], src, ident[:])
                    last.then_inc(s_T, 1)

                def values(u):
                    t, h = u // H, u % H
                    if t >= 2 and h == 0:
                        pe.wait_ge(s_o, t - 1)
                    pe.wait_ge(s_ptd, USER_OF["p", u] + 1)
                    if t >= 4:
                        pe.wait_ge(s_pta, ACT_OUT[USER_OF["p", u]])
                    for j in range(t + 1):
                        last = pe.matmul(ps[6 + t % 2][:, h * HD:(h + 1) * HD], PTS[:, u % 2, j], VS[:, j, h * HD:(h + 1) * HD], start=j == 0, stop=j == t)
                    last.then_inc(s_pv, 1)

                scores(0)
                scores(1)
                turn(0)
                pe.wait_ge(s_v, 16)
                for u in range(NU):
                    if u + 2 < NU:
                        scores(u + 2)
                    if u + 1 < NU:
                        turn(u + 1)
                    values(u)
                mixed(TT - 1)

    r4 = Region(A_RAW + 32 * KB, 16 * KB)
    wb4 = r4.take("wb4", [P, D])
    xr = r4.take("xr", [P, 2, D])
    h2T = r4.take("h2T", [P, KT, P])
    sqr4 = Region(A_RAW, 4 * KB).take("sqr4", [P, D])
    m8 = ext.take("m8", [P, TT, 8])
    pos = ext.take("pos", [P, TT * TOPK], u32)
    idxall = ext.take("idxall", [P, SBMAX + 1], u32)
    tab = ext.take("tab", [1, SSB + 1, 3], i32)
    nblk = ext.take("nblk", [1, 1], i32)
    E1 = ext.at
    r4e = Region(E1, left - (E1 - A_E))
    x1 = r4e.take("x1", [P, 2, D])
    h2 = r4e.take("h2", [P, 2, D])
    rw = r4e.take("rw", [P, KT, NE])
    rb = r4e.take("rb", [P, NE])
    logits = r4e.take("logits", [P, TT, NE])

    def stage4():
        def s4(n):
            return sem("s4_" + n)
        s_raw, s_wb, s_rw, s_x, s_st = [s4("raw0"), s4("raw1")], s4("wb"), s4("rw"), [s4("x0"), s4("x1")], [s4("st0"), s4("st1")]
        s_sh = [s4("sh0"), s4("sh1")]
        s_hi, s_w, s_out, s_x1, s_ss, s_rs, s_h2, s_T, s_h2T, s_l, s_lg = (s4(n) for n in ("hi", "w", "out", "x1d", "ss", "rs", "h2", "T", "h2T", "l", "lg"))

        with nc.Block() as block:
            @block.sync
            def _(sp):
                for c in range(2):
                    sp.dma_start(RAW[:, c], w_out[:, :, c * CH:(c + 1) * CH]).then_inc(s_raw[c], 16)
                sp.dma_start(wb4[:], A["moe_norm_w"][0].partition_broadcast(P)).then_inc(s_wb, 16)
                sp.dma_start(rw[:], A["router_w"][0].rearrange("(k p) e -> p k e", p=P)).then_inc(s_rw, 16)
                sp.dma_start(rb[:], A["router_b"][0].partition_broadcast(P)).then_inc(s_rw, 16)
                for t in range(TT + 1):
                    if t < TT:
                        if t >= 2:
                            sp.wait_ge(s_x1, t - 1)
                        sp.dma_start(xr[:, t % 2], x2[tok(t), :]).then_inc(s_x[t % 2], 16)
                    if t >= 1:
                        sp.wait_ge(s_x1, t)
                        sp.dma_start(dX1[tok(t - 1), :], x1[:, (t - 1) % 2]).then_inc(s_st[(t - 1) % 2], 16)
                        sp.wait_ge(s_h2, t)
                        sp.dma_start(dH2[tok(t - 1), :], h2[:, (t - 1) % 2]).then_inc(s_sh[(t - 1) % 2], 16)
                for i in range(2):
                    sp.wait_ge(s_st[i], 16 * TT // 2)
                    sp.wait_ge(s_sh[i], 16 * TT // 2)

            @block.gpsimd
            def _(pool):
                link = chain(pool, "s4_pool")
                for t in range(TT):
                    pool.wait_ge(s_ss, t + 1)
                    r = rmsB[:, t:t + 1]
                    inv_root(pool, link, r, r, D).then_inc(s_rs, 1)

            @block.scalar
            def _(act):
                for c in range(2):
                    act.wait_ge(s_raw[c], 16)
                    act.activation(WH[:, c], RAW[:, c], ACT.Copy).then_inc(s_hi, 1)
                act.wait_ge(s_w, 1)
                for t in range(TT + 1):
                    if t >= 1:
                        act.wait_ge(s_T, t)
                        if t >= 2:
                            act.wait_ge(s_l, t - 1)
                        act.activation(h2T[:].rearrange("p k c -> p (k c)"), pair(2, D), ACT.Copy).then_inc(s_h2T, 1)
                    if t < TT:
                        act.wait_ge(s_x1, t + 1)
                        if t >= 1:
                            act.wait_ge(s_ss, t)
                        act.activation(sqr4[:], x1[:, t % 2], ACT.Square, accum_out=rmsB[:, t:t + 1]).then_inc(s_ss, 1)

            @block.vector
            def _(dve):
                for c in range(2):
                    dve.wait_ge(s_hi, c + 1)
                    dve.tensor_tensor(WL[:, c], RAW[:, c], WH[:, c].bitcast(f32), ALU.subtract).then_inc(s_w, 1)
                dve.wait_ge(s_wb, 16)
                dve.wait_ge(s_rw, 32)
                for t in range(TT):
                    dve.wait_ge(s_out, t + 1)
                    dve.wait_ge(s_x[t % 2], 16 * (t // 2 + 1))
                    if t >= 2:
                        dve.wait_ge(s_st[t % 2], 16 * (t // 2))
                        dve.wait_ge(s_ss, t - 1)
                    dve.tensor_tensor(x1[:, t % 2], xr[:, t % 2], pair(t % 2, D), ALU.add).then_inc(s_x1, 1)
                    dve.wait_ge(s_rs, t + 1)
                    if t >= 2:
                        dve.wait_ge(s_sh[t % 2], 16 * (t // 2))
                        dve.wait_ge(s_T, t - 1)
                    dve.scalar_tensor_tensor(out=h2[:, t % 2], in0=x1[:, t % 2], scalar=rmsB[:, t:t + 1], in1=wb4[:],
                                             op0=ALU.mult, op1=ALU.mult).then_inc(s_h2, 1)
                    if t >= 1:
                        dve.wait_ge(s_l, t)
                        dve.tensor_tensor(logits[:, t - 1], ps[6 + (t - 1) % 2][:, 0:NE], rb[:], ALU.add).then_inc(s_lg, 1)
                dve.wait_ge(s_l, TT)
                dve.tensor_tensor(logits[:, TT - 1], ps[6 + (TT - 1) % 2][:, 0:NE], rb[:], ALU.add).then_inc(s_lg, 1)

            @block.tensor
            def _(pe):
                pe.wait_ge(s_rw, 32)

                def project(t, c):
                    pe.wait_ge(s_w, c + 1)
                    for k in range(KT):
                        last = mm3(pe, ps[2 * (t % 2) + c], XH[:, k, tok(t)], XL[:, k, tok(t)], WH[:, c, k], WL[:, c, k], k == 0, k == KT - 1)
                    return last

                for t in range(TT + 1):
                    if t < TT:
                        if t >= 2:
                            pe.wait_ge(s_x1, t - 1)
                        project(t, 0)
                    if t >= 1:
                        pe.wait_ge(s_h2, t)
                        if t >= 2:
                            pe.wait_ge(s_h2T, t - 1)
                        for k in range(KT):
                            last = pe.transpose(ps[4 + k // 4][:, (k % 4) * P:(k % 4 + 1) * P], h2[:, (t - 1) % 2, k * P:(k + 1) * P], ident[:])
                        last.then_inc(s_T, 1)
                    if t < TT:
                        project(t, 1).then_inc(s_out, 1)
                    if t >= 1:
                        pe.wait_ge(s_h2T, t)
                        if t >= 3:
                            pe.wait_ge(s_lg, t - 2)
                        for k in range(KT):
                            last = pe.matmul(ps[6 + (t - 1) % 2][:, 0:NE], h2T[:, k], rw[:, k], start=k == 0, stop=k == KT - 1)
                        last.then_inc(s_l, 1)

    r5 = Region(A_X + 96 * KB, 32 * KB)
    ix8 = r5.take("ix8", [P, TT, 8], u32)
    ixf = r5.take("ixf", [P, TT * TOPK])
    iotaE = r5.take("iotaE", [P, NE])
    sel = r5.take("sel", [P, TT * TOPK, NE])
    selS = r5.take("selS", [P, TT, NE])
    prod = r5.take("prod", [P, TT * TOPK, NE])
    posf = r5.take("posf", [P, TT * TOPK])
    rank = r5.take("rank", [P, TT, NE])
    tsum = r5.take("tsum", [P, TT + 1, NE])
    nb = r5.take("nb", [P, NE])
    be = r5.take("be", [P, NE])
    bs = r5.take("bs", [P, NE])
    le = r5.take("le", [P, NE])
    srow = r5.take("srow", [P, 1])
    ns = r5.take("ns", [P, NE])
    se = r5.take("se", [P, NE])
    hot = r5.take("hot", [P, NE])
    entf = r5.take("entf", [P, 4])
    enti = r5.take("enti", [P, 3], i32)
    nbi = r5.take("nbi", [P, 1], i32)
    onesE = r5.take("onesE", [P, NE])
    gsum = r5.take("gsum", [P, TT])
    g4 = ext.take("g4", [P, TT, TOPK])
    tokid = r5.take("tokid", [P, TT])
    zrow = r5.take("zrow", [P, P])
    tokr = r5.take("tokr", [P, P])

    def stage5():
        def s5(n):
            return sem("s5_" + n)
        s_it, s_sel, s_rank, s_pos, s_zd, s_sc, s_tk, s_tT, s_e = (s5(n) for n in ("iota", "sel", "rank", "pos", "zeroed", "scat", "tok", "tokT", "exp"))
        s_m, s_tab, s_tb, s_tb2, s_ix, s_z = s5("m"), s5("tabs"), s5("tabd"), s5("tabl"), s5("idx"), s5("z")

        with nc.Block() as block:
            @block.sync
            def _(sp):
                sp.wait_ge(s_z, 1)
                sp.dma_start(dTok.rearrange("(s p) a -> s (p a)", p=P), zrow[0:SBMAX]).then_inc(s_zd, 16)
                sp.wait_ge(s_tab, 1)
                sp.dma_start(dTab, enti[0:SSB + 1]).then_inc(s_tb, 16)
                sp.dma_start(dN, nbi[0:1]).then_inc(s_tb, 16)
                sp.wait_ge(s_tb, 32)
                sp.dma_start(tab[0:1].rearrange("a s j -> a (s j)"), dTab.rearrange("(a s) j -> a (s j)", a=1)).then_inc(s_tb2, 16)
                sp.dma_start(nblk[:], dN).then_inc(s_tb2, 16)
                sp.wait_ge(s_tb2, 32)
                e0 = sp.value_load(tab[0:1, 0, 0:1], min_val=0, max_val=NE - 1)
                load(sp, 0, e0)
                bias(sp, 0, e0)
                bias(sp, 1, e0)
                load(sp, 1, e0)
                load(sp, 2, e0)
                sp.wait_ge(s_sc, 16 * TT * TOPK)
                sp.dma_start(tokr[0:SBMAX], dTok.rearrange("(s p) a -> s (p a)", p=P)).then_inc(s_tk, 16)

            @block.gpsimd
            def _(pool):
                pool.memset(zrow[:], 0.0).then_inc(s_z, 1)
                pool.iota(iotaE[:], pattern=[[1, NE]], base=0, channel_multiplier=0, allow_small_or_imprecise_dtypes=True)
                pool.iota(srow[:], pattern=[[1, 1]], base=0, channel_multiplier=1, allow_small_or_imprecise_dtypes=True)
                pool.iota(tokid[:], pattern=[[P, TT]], base=0, channel_multiplier=1, allow_small_or_imprecise_dtypes=True).then_inc(s_it, 1)
                pool.wait_ge(s_it, 1)
                pool.wait_ge(s_pos, 1)
                pool.wait_ge(s_zd, 16)
                for i in range(TT * TOPK):
                    pool.indirect_dma_start(dTok, bass.IndirectOffsetOnAxis(ap=pos[:, i:i + 1], axis=0),
                                            tokid[:, i // TOPK:i // TOPK + 1], None).then_inc(s_sc, 16)
                pool.wait_ge(s_b[0], 16)
                spread(pool, 0)
                for c in range(3):
                    pool.wait_ge(s_hi, 2 * c + 2)
                    pool_split(pool, c)
                pool.wait_ge(s_sc, 16 * TT * TOPK)

            @block.scalar
            def _(act):
                act.wait_ge(s_m, 1)
                act.activation(g4[:], g4[:], ACT.Exp).then_inc(s_e, 1)
                for c in range(3):
                    act.wait_ge(s_raw[c], 32)
                    split_hi(act, c, 0)
                    split_hi(act, c, 1)

            @block.vector
            def _(dve):
                link = chain(dve, "s5_dve")
                for t in range(TT):
                    link(dve.max(m8[:, t], logits[:, t]))
                    link(dve.max_index(ix8[:, t], m8[:, t], logits[:, t]))
                dve.tensor_tensor(g4[:], m8[:, :, 0:TOPK], bc(m8[:, :, 0:1], [P, TT, TOPK]), ALU.subtract).then_inc(s_m, 1)
                link(dve.tensor_copy(ixf[:].rearrange("p (t k) -> p t k", k=TOPK), ix8[:, :, 0:TOPK]))
                dve.wait_ge(s_it, 1)
                link(dve.tensor_tensor(sel[:], bc(iotaE[:].unsqueeze(1), [P, TT * TOPK, NE]), bc(ixf[:].unsqueeze(2), [P, TT * TOPK, NE]), ALU.is_equal))
                dve.tensor_reduce(selS[:], sel[:].rearrange("p (t k) e -> p t e k", k=TOPK), X, ALU.add).then_inc(s_sel, 1)
                dve.memset(onesE[:], 1.0)
                dve.memset(tsum[:, 0], 0.0)
                dve.wait_ge(s_rank, 1)
                link(dve.tensor_copy(tsum[:, 1], ps[1][:, 0:NE]))
                for t in range(1, TT):
                    link(dve.tensor_tensor(tsum[:, t + 1], tsum[:, t], ps[1][:, t * NE:(t + 1) * NE], ALU.add))
                cnt = tsum[:, TT]
                link(dve.tensor_scalar(nb[:], cnt, 0.0, None, ALU.is_gt))
                for j in range(1, S // P):
                    link(dve.scalar_tensor_tensor(out=nb[:], in0=cnt, scalar=float(j * P), in1=nb[:], op0=ALU.is_gt, op1=ALU.add))
                link(dve.tensor_tensor_scan(be[:], onesE[:], nb[:], 0.0, ALU.mult, ALU.add))
                link(dve.tensor_tensor(bs[:], be[:], nb[:], ALU.subtract))
                link(dve.scalar_tensor_tensor(out=rank[:], in0=bc(bs[:].unsqueeze(1), [P, TT, NE]), scalar=float(P), in1=ps[0][:, 0:TT * NE].rearrange("p (t e) -> p t e", e=NE), op0=ALU.mult, op1=ALU.add))
                link(dve.tensor_tensor(rank[:], rank[:], tsum[:, 0:TT], ALU.add))
                for k in range(TOPK):
                    last = dve.tensor_tensor(prod[:].rearrange("p (t k) e -> p t k e", k=TOPK)[:, :, k], sel[:].rearrange("p (t k) e -> p t k e", k=TOPK)[:, :, k], rank[:], ALU.mult)
                link(last)
                link(dve.tensor_reduce(posf[:], prod[:], X, ALU.add))
                dve.tensor_copy(pos[:], posf[:]).then_inc(s_pos, 1)
                link(dve.tensor_scalar(ns[:], nb[:], 0.0, None, ALU.is_gt))
                for j in range(2, S // P, 2):
                    link(dve.scalar_tensor_tensor(out=ns[:], in0=nb[:], scalar=float(j), in1=ns[:], op0=ALU.is_gt, op1=ALU.add))
                link(dve.tensor_tensor_scan(se[:], onesE[:], ns[:], 0.0, ALU.mult, ALU.add))
                link(dve.tensor_scalar(le[:], se[:], srow[:, 0:1], None, ALU.is_le))
                link(dve.tensor_reduce(entf[:, 0:1], le[:], X, ALU.add))
                link(dve.tensor_scalar(entf[:, 0:1], entf[:, 0:1], float(NE - 1), None, ALU.min))
                link(dve.tensor_scalar(hot[:], iotaE[:], entf[:, 0:1], None, ALU.is_equal))
                link(dve.tensor_tensor(ns[:], ns[:], se[:], ALU.subtract))
                link(dve.scalar_tensor_tensor(out=ns[:], in0=ns[:], scalar=2.0, in1=bs[:], op0=ALU.mult, op1=ALU.add))
                link(dve.scalar_tensor_tensor(out=ns[:], in0=srow[:, 0:1].broadcast_to([P, NE]), scalar=2.0, in1=ns[:], op0=ALU.mult, op1=ALU.add))
                link(dve.tensor_tensor(ns[:], ns[:], hot[:], ALU.mult))
                link(dve.tensor_reduce(entf[:, 1:2], ns[:], X, ALU.add))
                link(dve.tensor_tensor(hot[:], be[:], hot[:], ALU.mult))
                link(dve.tensor_reduce(entf[:, 3:4], hot[:], X, ALU.add))
                link(dve.tensor_tensor(entf[:, 2:3], entf[:, 3:4], entf[:, 1:2], ALU.subtract))
                link(dve.tensor_scalar(entf[:, 2:3], entf[:, 2:3], 1.5, None, ALU.is_gt))
                link(dve.tensor_scalar(entf[:, 1:2], entf[:, 1:2], float(SBMAX - 1), None, ALU.min))
                dve.tensor_copy(enti[:], entf[:, 0:3])
                dve.tensor_copy(nbi[:], se[:, NE - 1:NE]).then_inc(s_tab, 1)
                dve.wait_ge(s_e, 1)
                link(dve.tensor_reduce(gsum[:], g4[:], X, ALU.add))
                link(dve.reciprocal(gsum[:], gsum[:]))
                dve.tensor_tensor(g4[:], g4[:], bc(gsum[:].unsqueeze(2), [P, TT, TOPK]), ALU.mult)
                dve.memset(idxall[:, SBMAX:SBMAX + 1], 0)
                for c in range(3):
                    split_lo(dve, c, 0, 2 * c + 1)
                    if c < 2:
                        split_lo(dve, c, 1, 2 * c + 2)
                dve.wait_ge(s_tT, 1)
                dve.tensor_copy(idxall[:, 0:SBMAX], ps[2][:, 0:SBMAX]).then_inc(s_ix, 1)

            @block.tensor
            def _(pe):
                pe.wait_ge(s_sel, 1)
                every = selS[:].rearrange("p t e -> p (t e)")
                pe.matmul(ps[0][:, 0:TT * NE], before[:], every, start=True, stop=True)
                pe.matmul(ps[1][:, 0:TT * NE], ones[:], every, start=True, stop=True).then_inc(s_rank, 1)
                pe.wait_ge(s_tk, 16)
                pe.transpose(ps[2][:, 0:SBMAX], tokr[0:SBMAX], ident[0:SBMAX, 0:SBMAX]).then_inc(s_tT, 1)

    w_gu = A["expert_w_gate_up"][0].rearrange("e (k p) n -> e p k n", p=P)
    w_dn = A["expert_w_down"][0].rearrange("e (k p) n -> e p k n", p=P)
    b_gu, b_dn = A["expert_b_gate_up"][0], A["expert_b_down"][0]
    r6 = Region(A_X, 128 * KB)
    VH = r6.take("VH", [P, 3, KT, CH], f32r)
    VL = r6.take("VL", [P, 3, KT, CH], f32r)
    TH = r6.take("TH", [P, 2, KT, P], f32r)
    TL = r6.take("TL", [P, 2, KT, P], f32r)
    AH = r6.take("AH", [P, 2, KT, P], f32r)
    AL = r6.take("AL", [P, 2, KT, P], f32r)
    r6e = Region(ext.at, nc.sbuf_usable_end - ext.at)
    gu = r6e.take("gu", [P, 2, CH])
    r6t = Region(A_TR, 4 * KB)
    sg = r6t.take("sg", [P, 2, HC])
    qa = r6t.take("qa", [P, 2, HC])
    brow = r6e.take("brow", [1, 2, CH])
    bb = r6e.take("bb", [P, 2, CH])
    xg = r6e.take("xg", [P, 2, D])
    icur = r6e.take("icur", [P, 2], u32)
    warm = r6e.take("warm", [P, 1])
    HK = KT // 2
    KP = 1

    s_raw = [nc.alloc_semaphore(f"s6_raw{i}") for i in range(3)]
    s_hi, s_w = nc.alloc_semaphore("s6_hi"), nc.alloc_semaphore("s6_w")
    s_wp = nc.alloc_semaphore("s6_wp")
    s_b = [nc.alloc_semaphore(f"s6_bias{i}") for i in range(2)]
    s_bb = nc.alloc_semaphore("s6_bb")

    def load(sp, c, e):
        for g in range(2):
            if c < GU:
                dst = RAW[:, c % 3, :, g * HC:(g + 1) * HC]
                src = w_gu[bass.ds(e, 1), :, :, g * D + c * HC:g * D + (c + 1) * HC]
            else:
                dst = RAW[:, c % 3, g * HK:(g + 1) * HK]
                src = w_dn[bass.ds(e, 1), :, g * HK:(g + 1) * HK, (c - GU) * CH:(c - GU + 1) * CH]
            sp.dma_start(dst, src.rearrange("a p k n -> p (a k) n")).then_inc(s_raw[c % 3], 16)

    def bias(sp, c, e):
        if c < GU:
            src = b_gu[bass.ds(e, 1), :].rearrange("a (g n) -> a g n", g=2)[:, :, c * HC:(c + 1) * HC]
            dst = brow[0:1, c % 2].rearrange("a (g n) -> a g n", g=2)
        else:
            src, dst = b_dn[bass.ds(e, 1), (c - GU) * CH:(c - GU + 1) * CH], brow[0:1, c % 2]
        sp.dma_start(dst, src).then_inc(s_b[c % 2], 16)

    def spread(pool, c):
        pool.partition_broadcast(bb[:, c % 2], brow[0:1, c % 2], P).then_inc(s_bb, 1)

    def pool_split(pool, i):
        ks = slice(KT - KP, KT)
        pool.tensor_tensor(VL[:, i, ks], RAW[:, i, ks], VH[:, i, ks].bitcast(f32), ALU.subtract).then_inc(s_wp, 1)

    def split_hi(act, i, hf):
        ks = slice(hf * HK, (hf + 1) * HK)
        act.activation(VH[:, i, ks], RAW[:, i, ks], ACT.Copy).then_inc(s_hi, 1)

    def split_lo(dve, i, hf, rounded):
        dve.wait_ge(s_hi, rounded)
        ks = slice(hf * HK, (hf + 1) * HK - (KP if hf else 0))
        dve.tensor_tensor(VL[:, i, ks], RAW[:, i, ks], VH[:, i, ks].bitcast(f32), ALU.subtract).then_inc(s_w, 1)

    def stage6():
        def s6(n):
            return sem("s6_" + n)
        s_mm, s_ev = s6("mm"), s6("ev")
        s_waited = s6("waited")
        s_ic, s_xg, s_xT, s_xhi, s_x = s6("ic"), [s6("xg0"), s6("xg1")], s6("xT"), s6("xhi"), s6("x")
        s_g, s_up, s_sg, s_q = s6("g"), s6("up"), s6("sg"), s6("q")
        s_a, s_aT, s_ahi, s_act = s6("a"), s6("aT"), s6("ahi"), s6("act")
        s_st, s_y0, s_warm = [s6("st0"), s6("st1")], s6("y0"), s6("warm")
        held.extend([*s_raw, s_hi, s_w, s_wp, *s_b, s_bb])
        G2, N2 = 2 * GU, 2 * NCH

        def items(c, nh):
            return [(h, c * nh + h) for h in range(nh)]

        def superblocks(eng, body):
            n = eng.value_load(nblk[0:1, 0:1], min_val=1, max_val=SSB)
            with eng.Fori(0, SSB) as s:
                with eng.If(s < n):
                    two = eng.value_load(tab[0:1, bass.ds(s, 1), 2:3], min_val=0, max_val=1)
                    with eng.If(two > 0):
                        body(s, 2)
                    with eng.Else():
                        body(s, 1)
                with eng.Else():
                    eng.nop()
            return n

        with nc.Block() as block:
            @block.sync
            def _(sp):
                def wait(s_, value):
                    sp.wait_ge(s_, value)
                    sp.sem_inc(s_waited, 1)

                def body(s, nh):
                    e = sp.value_load(tab[0:1, bass.ds(s, 1), 0:1], min_val=0, max_val=NE - 1)
                    en = sp.value_load(tab[0:1, bass.ds(s + 1, 1), 0:1], min_val=0, max_val=NE - 1)
                    fb = sp.value_load(tab[0:1, bass.ds(s, 1), 1:2], min_val=0, max_val=SBMAX - nh)
                    for c in range(NCH):
                        wait(s_bb, s * NCH + (c + 2))
                        bias(sp, (c + 3) % NCH, e if c + 3 < NCH else en)
                        if c >= GU:
                            for h, i in items(c, nh):
                                wait(s_ev, s * N2 + (2 * c + (h + 1) * 2 // nh + 4))
                                rows = bass.ds(fb * P + h * P, P)
                                for q in range(2 // nh):
                                    cols = slice(q * HC, (q + 1) * HC) if nh == 1 else slice(0, CH)
                                    at = (c - GU) * CH + cols.start
                                    sp.dma_start(dY[rows, at:at + cols.stop - cols.start], gu[:, i % 2, cols]).then_inc(s_st[i % 2], 16)
                        wait(s_w, s * N2 + (2 * (c + 2) + 2))
                        wait(s_wp, s * NCH + (c + 3))
                        load(sp, (c + 5) % NCH, e if c == 0 else en)

                e0 = sp.value_load(tab[0:1, 0, 0:1], min_val=0, max_val=NE - 1)
                sp.wait_ge(s_y0, 1)
                for j in range(2):
                    sp.dma_start(dY[0:P, j * CH:(j + 1) * CH], gu[:, j]).then_inc(s_st[j], 16)
                sp.wait_ge(s_bb, 1)
                bias(sp, 2, e0)
                for c in range(2):
                    sp.wait_ge(s_w, 2 * c + 2)
                    sp.wait_ge(s_wp, c + 1)
                    load(sp, c + 3, e0)
                n = superblocks(sp, body)
                for i in range(3):
                    wait(s_raw[i], n * 64 + (64 if i < 2 else 32))
                for i in range(2):
                    wait(s_b[i], n * 48 + (32 - 16 * i))
                    wait(s_st[i], n * 32 + 16)

            @block.gpsimd
            def _(pool):
                def wait(s_, value):
                    pool.wait_ge(s_, value)
                    pool.sem_inc(s_waited, 1)

                def gather():
                    for h in range(2):
                        pool.indirect_dma_start(xg[:, h], None, dH2, bass.IndirectOffsetOnAxis(ap=icur[:, h:h + 1], axis=0)).then_inc(s_xg[h], 16)

                def body(s, nh):
                    fb = pool.value_load(tab[0:1, bass.ds(s + 1, 1), 1:2], min_val=0, max_val=SBMAX - 1)
                    for c in range(NCH):
                        n = c + 1
                        wait(s_ev, s * N2 + (2 * c + 4))
                        wait(s_b[n % 2], s * 48 + 16 * (n // 2 + 1))
                        spread(pool, n)
                        if c < GU:
                            for h, i in items(c, nh):
                                w = 2 // nh
                                wait(s_ev, s * N2 + (2 * c + (h + 1) * w + 4))
                                pool.tensor_scalar(gu[:, i % 2, HC:CH], gu[:, i % 2, HC:CH], LIMIT, -LIMIT, ALU.min, ALU.max).then_inc(s_up, w)
                        wait(s_hi, s * N2 + (2 * (c + 3) + 2))
                        pool_split(pool, c % 3)
                        if c == 0:
                            wait(s_xT, s * 2 + 2)
                            wait(s_xg[1], s * 16 + 16)
                            pool.tensor_copy(icur[:], idxall[:, bass.ds(fb, 2)]).then_inc(s_ic, 1)
                            wait(s_ic, s + 2)
                            gather()

                pool.tensor_copy(icur[:], idxall[:, 0:2]).then_inc(s_ic, 1)
                pool.wait_ge(s_ic, 1)
                gather()
                n = superblocks(pool, body)
                wait(s_xg[0], n * 16 + 16)
                wait(s_xg[1], n * 16 + 16)

            @block.scalar
            def _(act):
                def tokens_hi(h):
                    act.activation(TH[:, h].rearrange("p k c -> p (k c)"), pair(3, D), ACT.Copy).then_inc(s_xhi, 1)

                def act_hi(s, i, nh):
                    c, h, w = i // nh, i % nh, 2 // nh
                    act.wait_ge(s_aT, s * G2 + (i + 1) * w)
                    act.activation(AH[:, h, 2 * c:2 * c + 2].rearrange("p k c -> p (k c)"), ps[4 + i % 2][:, 0:HC], ACT.Copy).then_inc(s_ahi, w)

                def body(s, nh):
                    w = 2 // nh
                    act.wait_ge(s_warm, s + 1)
                    act.activation(warm[:], onec[:], ACT.Sigmoid).then_inc(s_warm, 1)
                    if nh == 2:
                        act.wait_ge(s_xT, s * 2 + 2)
                        tokens_hi(1)
                    else:
                        act.wait_ge(s_xT, s * 2 + 2)
                        act.sem_inc(s_xhi, 1)
                    for c in range(NCH):
                        for h, i in items(c, nh):
                            if c == GU and h == 0:
                                act.wait_ge(s_xT, s * 2 + 3)
                                tokens_hi(0)
                            if 1 <= i < GU * nh:
                                act_hi(s, i - 1, nh)
                            if c < GU:
                                act.wait_ge(s_g, s * G2 + (i + 1) * w)
                                act.activation(sg[:, i % 2], gu[:, i % 2, 0:HC], ACT.Sigmoid, scale=ALPHA).then_inc(s_sg, w)
                            if h == nh - 1:
                                act.wait_ge(s_mm, s * N2 + (2 * c + 2))
                                act.wait_ge(s_raw[c % 3], s * 64 + 32 * ((c + 3) // 3 + 1))
                                split_hi(act, c % 3, 0)
                                if c == GU - 1:
                                    act_hi(s, i, nh)
                                split_hi(act, c % 3, 1)

                act.wait_ge(s_xT, 1)
                tokens_hi(0)
                act.activation(warm[:], onec[:], ACT.Copy).then_inc(s_warm, 1)
                superblocks(act, body)

            @block.vector
            def _(dve):
                def tokens_lo(h, count):
                    dve.wait_ge(s_xhi, count)
                    dve.tensor_tensor(TL[:, h].rearrange("p k c -> p (k c)"), pair(3, D), TH[:, h].rearrange("p k c -> p (k c)").bitcast(f32), ALU.subtract).then_inc(s_x, 1)

                def act_lo(s, i, nh):
                    c, h, w = i // nh, i % nh, 2 // nh
                    dve.wait_ge(s_ahi, s * G2 + (i + 1) * w)
                    dve.tensor_tensor(AL[:, h, 2 * c:2 * c + 2].rearrange("p k c -> p (k c)"), ps[4 + i % 2][:, 0:HC],
                                      AH[:, h, 2 * c:2 * c + 2].rearrange("p k c -> p (k c)").bitcast(f32), ALU.subtract).then_inc(s_act, w)

                def body(s, nh):
                    w = 2 // nh
                    if nh == 2:
                        tokens_lo(1, s * 2 + 2)
                    else:
                        dve.wait_ge(s_xhi, s * 2 + 2)
                        dve.sem_inc(s_x, 1)
                    for c in range(NCH):
                        for h, i in items(c, nh):
                            b = i % 2
                            if c == GU and h == 0:
                                tokens_lo(0, s * 2 + 3)
                            dve.wait_ge(s_a, s * G2 + (2 + min(G2, max(0, i - 1) * w)))
                            if i < 2:
                                dve.wait_ge(s_st[b], s * 32 + 16)
                            elif i - 2 >= GU * nh:
                                dve.wait_ge(s_st[b], s * 32 + 32)
                            dve.wait_ge(s_mm, s * N2 + (i + 1) * w)
                            dve.wait_ge(s_bb, s * NCH + (c + 1))
                            dve.tensor_tensor(gu[:, b], ps[2 * (c % 2) + h], bb[:, c % 2], ALU.add).then_inc(s_ev, w)
                            if c < GU:
                                dve.wait_ge(s_ev, s * N2 + ((i + 1) * w + 4))
                                dve.tensor_scalar(gu[:, b, 0:HC], gu[:, b, 0:HC], LIMIT, None, ALU.min).then_inc(s_g, w)
                            if 1 <= i < GU * nh:
                                act_lo(s, i - 1, nh)
                            if h == 0 and c != GU - 1:
                                split_lo(dve, (c + 2) % 3, 1, s * N2 + (2 * (c + 2) + 2))
                            if c < GU:
                                dve.wait_ge(s_sg, s * G2 + (i + 1) * w)
                                dve.tensor_tensor(sg[:, b], gu[:, b, 0:HC], sg[:, b], ALU.mult).then_inc(s_q, w)
                                dve.wait_ge(s_q, s * G2 + (i + 1) * w)
                                dve.wait_ge(s_up, s * G2 + (i + 1) * w)
                                dve.scalar_tensor_tensor(out=qa[:, b], in0=gu[:, b, HC:CH], scalar=1.0, in1=sg[:, b], op0=ALU.add, op1=ALU.mult).then_inc(s_a, w)
                            if h == 0 and c == GU - 1:
                                split_lo(dve, (c + 2) % 3, 1, s * N2 + (2 * (c + 2) + 2))
                            if h == nh - 1:
                                if c == GU - 1:
                                    act_lo(s, i, nh)
                                split_lo(dve, c % 3, 0, s * N2 + (2 * (c + 3) + 1))

                dve.memset(gu[:], 0.0).then_inc(s_y0, 1)
                dve.sem_inc(s_a, 2)
                dve.sem_inc(s_ev, 4)
                dve.sem_inc(s_act, 2)
                tokens_lo(0, 1)
                superblocks(dve, body)

            @block.tensor
            def _(pe):
                def tokens(h, arrived, taken=None):
                    pe.wait_ge(s_xg[h], arrived)
                    if taken is not None:
                        pe.wait_ge(s_x, taken)
                    for k in range(KT):
                        last = pe.transpose(ps[6 + k // 4][:, (k % 4) * P:(k % 4 + 1) * P], xg[:, h, k * P:(k + 1) * P], ident[:])
                    last.then_inc(s_xT, 1)

                def product(s, o, c, lh, ll, ks):
                    for k in ks:
                        if k % HK == 0:
                            pe.wait_ge(s_w, s * N2 + (2 * c + 1 + k // HK))
                        if k == KT - KP:
                            pe.wait_ge(s_wp, s * NCH + (c + 1))
                        last = mm3(pe, o, lh[:, k], ll[:, k], VH[:, c % 3, k], VL[:, c % 3, k], k == 0, k == KT - 1)
                    return last

                def turned(s, i, nh):
                    w = 2 // nh
                    pe.wait_ge(s_a, s * G2 + (2 + (i + 1) * w))
                    pe.wait_ge(s_act, s * G2 + (2 + max(0, i - 1) * w))
                    for j in range(2):
                        last = pe.transpose(ps[4 + i % 2][:, j * P:(j + 1) * P], qa[:, i % 2, j * P:(j + 1) * P], ident[:])
                    last.then_inc(s_aT, w)

                def body(s, nh):
                    w = 2 // nh
                    if nh == 2:
                        tokens(1, s * 16 + 16, s * 2 + 1)
                    else:
                        pe.wait_ge(s_x, s * 2 + 1)
                        pe.sem_inc(s_xT, 1)
                    for c in range(NCH):
                        if c == GU:
                            tokens(0, s * 16 + 32, s * 2 + 2)
                        pe.wait_ge(s_ev, s * N2 + (2 * c + 2))
                        for h, i in items(c, nh):
                            o = ps[2 * (c % 2) + h]
                            if i == 1 and c == 0:
                                pe.wait_ge(s_x, s * 2 + 2)
                            if c < GU:
                                product(s, o, c, TH[:, h], TL[:, h], range(KT)).then_inc(s_mm, w)
                                if i >= 1:
                                    turned(s, i - 1, nh)
                            elif i == GU * nh:
                                pe.wait_ge(s_act, s * G2 + (2 + ((GU - 3) * nh + 1) * w))
                                product(s, o, c, AH[:, h], AL[:, h], range(HK))
                                turned(s, i - 1, nh)
                                pe.wait_ge(s_act, s * G2 + (2 + ((GU - 2) * nh + 1) * w))
                                product(s, o, c, AH[:, h], AL[:, h], range(HK, KT - 2))
                                pe.wait_ge(s_act, s * G2 + (2 + ((GU - 1) * nh + 1) * w))
                                product(s, o, c, AH[:, h], AL[:, h], range(KT - 2, KT)).then_inc(s_mm, w)
                            else:
                                pe.wait_ge(s_act, s * G2 + (2 + G2))
                                product(s, o, c, AH[:, h], AL[:, h], range(KT)).then_inc(s_mm, w)

                tokens(0, 16)
                superblocks(pe, body)

    YR = 4
    r7 = Region(A_X, 128 * KB)
    yk = r7.take("yk", [P, YR, TOPK, D])
    acc = r7.take("acc", [P, TT, D])

    def stage7():
        def s7(n):
            return sem("s7_" + n)
        s_x, s_k, s_a, s_o = [s7("x0"), s7("x1")], [s7(f"y{i}") for i in range(YR)], s7("acc"), s7("out")

        with nc.Block() as block:
            @block.sync
            def _(sp):
                for t in range(TT):
                    if t >= 2:
                        sp.wait_ge(s_x[t % 2], 16 * (t // 2))
                    sp.dma_start(acc[:, t], dX1[tok(t), :]).then_inc(s_x[t % 2], 16)
                for t in range(TT):
                    sp.wait_ge(s_a, TOPK * (t + 1))
                    sp.dma_start(out2[tok(t), :], acc[:, t]).then_inc(s_o, 16)
                sp.wait_ge(s_o, 16 * TT)

            @block.gpsimd
            def _(pool):
                for t in range(TT):
                    if t >= YR:
                        pool.wait_ge(s_a, TOPK * (t - YR + 1))
                    for k in range(TOPK):
                        pool.indirect_dma_start(yk[:, t % YR, k], None, dY, bass.IndirectOffsetOnAxis(ap=pos[:, t * TOPK + k:t * TOPK + k + 1], axis=0)).then_inc(s_k[t % YR], 16)

            @block.vector
            def _(dve):
                for t in range(TT):
                    dve.wait_ge(s_x[t % 2], 16 * (t // 2 + 1))
                    dve.wait_ge(s_k[t % YR], 16 * TOPK * (t // YR + 1))
                    for k in range(TOPK):
                        dve.scalar_tensor_tensor(out=acc[:, t], in0=yk[:, t % YR, k], scalar=g4[:, t, k:k + 1], in1=acc[:, t],
                                                 op0=ALU.mult, op1=ALU.add).then_inc(s_a, 1)
                        dve.wait_ge(s_a, TOPK * t + k + 1)


    for stage_ in (stage1, stage2, stage3, stage4, stage5, stage6, stage7):
        run(stage_)


_INS = ["x", "attn_norm_w", "w_in", "fox_f_bias", "fox_q_norm_w", "fox_k_norm_w", "fox_out_norm_w", "mlstm_conv_w",
        "mlstm_i_bias", "mlstm_f_bias", "mlstm_out_norm_w", "w_out", "moe_norm_w", "router_w", "router_b",
        "expert_w_gate_up", "expert_b_gate_up", "expert_w_down", "expert_b_down"]


def kernel(**inputs):
    import numpy as _np
    import concourse.bacc as _bacc
    from concourse import mybir as _mybir
    from concourse.bass_utils import run_bass_kernel_spmd as _run

    nc = _bacc.Bacc("TRN2", target_bir_lowering=False, num_devices=1)
    arrays, args = {}, {}
    for name in _INS:
        a = _np.ascontiguousarray(inputs[name])
        arrays[f"in_{name}"] = a
        args[name] = nc.dram_tensor(f"in_{name}", a.shape, _mybir.dt.from_np(a.dtype), kind="ExternalInput").ap()
    out = nc.dram_tensor("out_0", (1, S, D), _mybir.dt.float32, kind="ExternalOutput").ap()
    layer_kernel(nc, args, out)
    r = _run(nc, [arrays], core_ids=[0])
    return r.results[0]["out_0"]
```
